# Optimizing a Trainium2 kernel written in Bass

```python
import jax, jax.numpy as jnp
from jax import lax
import numpy as np

D_MODEL = 1024
BATCH = 1
SEQ = 2048
DEPTH = 2

N_META = 16
BLOCK = 128
ROPE_THETA = 10000.0
NORM_EPS = 1e-6
NEG_INF = -1e30

A_HEADS = 16
A_KV_HEADS = 2
A_HEAD_DIM = D_MODEL // A_HEADS
A_GROUP = A_HEADS // A_KV_HEADS
A_WINDOW = 128
A_Q_W = A_HEADS * A_HEAD_DIM
A_KV_W = A_KV_HEADS * A_HEAD_DIM
A_QKV = A_Q_W + 2 * A_KV_W

B_HEADS = 16
B_NOPE = 64
B_ROPE = 32
B_V = 64
B_Q_RANK = D_MODEL // 4
B_KV_RANK = D_MODEL // 8
B_IN = B_Q_RANK + B_KV_RANK + B_ROPE

N_GROUPS = 4
EXPERTS_PER_GROUP = 8
N_EXPERTS = N_GROUPS * EXPERTS_PER_GROUP
TOP_K = 2
D_EXPERT = D_MODEL // 4
MOE_BLOCK = 128

N_A_LAYERS = (DEPTH + 1) // 2
N_B_LAYERS = DEPTH // 2

kernel_name = "hybrid_swa_sink_mla_hier_moe_meta"

def rms_norm(x, g):
    xf = x.astype(jnp.float32)
    y = xf * lax.rsqrt(jnp.mean(xf * xf, axis=-1, keepdims=True) + NORM_EPS)
    return (y * g.astype(jnp.float32)).astype(x.dtype)

def rope_tables(length, dim):
    inv_freq = 1.0 / (ROPE_THETA ** (jnp.arange(0, dim, 2, dtype=jnp.float32) / dim))
    ang = jnp.arange(length, dtype=jnp.float32)[:, None] * inv_freq[None, :]
    return jnp.cos(ang), jnp.sin(ang)

def apply_rope(x, cos, sin):
    half = x.shape[-1] // 2
    xf = x.astype(jnp.float32)
    x1, x2 = xf[..., :half], xf[..., half:]
    return jnp.concatenate([x1 * cos - x2 * sin, x2 * cos + x1 * sin], axis=-1).astype(x.dtype)

def sink_softmax(s, sink):
    m = jnp.maximum(jnp.max(s, axis=-1, keepdims=True), sink)
    p = jnp.exp(s - m)
    return p / (jnp.sum(p, axis=-1, keepdims=True) + jnp.exp(sink - m))

def swa_sink_attention(h, w_qkv, b_qkv, sinks, w_o, b_o):
    B, L, _ = h.shape
    n_blk = (L - N_META) // BLOCK
    qkv = h @ w_qkv + b_qkv
    q = qkv[..., :A_Q_W].reshape(B, L, A_KV_HEADS, A_GROUP, A_HEAD_DIM)
    k = qkv[..., A_Q_W:A_Q_W + A_KV_W].reshape(B, L, A_KV_HEADS, A_HEAD_DIM)
    v = qkv[..., A_Q_W + A_KV_W:].reshape(B, L, A_KV_HEADS, A_HEAD_DIM)
    cos, sin = rope_tables(L, A_HEAD_DIM)
    q = apply_rope(q, cos[:, None, None], sin[:, None, None]) * (A_HEAD_DIM ** -0.5)
    k = apply_rope(k, cos[:, None], sin[:, None])
    sink = sinks.astype(jnp.float32).reshape(A_KV_HEADS, A_GROUP, 1, 1)

    qm, km, vm = q[:, :N_META], k[:, :N_META], v[:, :N_META]
    causal_m = jnp.tril(jnp.ones((N_META, N_META), dtype=bool))
    s_m = jnp.einsum('bqkgd,bskd->bkgqs', qm, km).astype(jnp.float32)
    p_m = sink_softmax(jnp.where(causal_m, s_m, NEG_INF), sink).astype(v.dtype)
    o_m = jnp.einsum('bkgqs,bskd->bqkgd', p_m, vm).reshape(B, N_META, A_Q_W)

    qr = q[:, N_META:].reshape(B, n_blk, BLOCK, A_KV_HEADS, A_GROUP, A_HEAD_DIM)
    kr = k[:, N_META:].reshape(B, n_blk, BLOCK, A_KV_HEADS, A_HEAD_DIM)
    vr = v[:, N_META:].reshape(B, n_blk, BLOCK, A_KV_HEADS, A_HEAD_DIM)

    def band(t, t_meta):
        prev = jnp.concatenate([jnp.zeros_like(t[:, :1]), t[:, :-1]], axis=1)
        meta = jnp.broadcast_to(t_meta[:, None], (B, n_blk) + t_meta.shape[1:])
        return jnp.concatenate([meta, prev, t], axis=2)

    kb, vb = band(kr, km), band(vr, vm)
    i = jnp.arange(BLOCK)[:, None]
    j = jnp.arange(BLOCK)[None, :]
    blk = jnp.arange(n_blk)[:, None, None]
    prev_ok = ((BLOCK + i - j) < A_WINDOW)[None] & (blk > 0)
    cur_ok = ((j <= i) & ((i - j) < A_WINDOW))[None]
    mask = jnp.concatenate([
        jnp.ones((n_blk, BLOCK, N_META), dtype=bool),
        jnp.broadcast_to(prev_ok, (n_blk, BLOCK, BLOCK)),
        jnp.broadcast_to(cur_ok, (n_blk, BLOCK, BLOCK))], axis=-1)
    s = jnp.einsum('bnqkgd,bnskd->bnkgqs', qr, kb).astype(jnp.float32)
    p = sink_softmax(jnp.where(mask[:, None, None], s, NEG_INF), sink).astype(v.dtype)
    o_r = jnp.einsum('bnkgqs,bnskd->bnqkgd', p, vb).reshape(B, n_blk * BLOCK, A_Q_W)

    o = jnp.concatenate([o_m, o_r], axis=1)
    return o @ w_o + b_o

def mla_attention(h, w_in, q_norm, kv_norm, w_uq, w_ukv, w_o):
    B, L, _ = h.shape
    n_blk = (L - N_META) // BLOCK
    c = h @ w_in
    c_q = c[..., :B_Q_RANK]
    c_kv = c[..., B_Q_RANK:B_Q_RANK + B_KV_RANK]
    k_pe = c[..., B_Q_RANK + B_KV_RANK:]
    q = (rms_norm(c_q, q_norm) @ w_uq).reshape(B, L, B_HEADS, B_NOPE + B_ROPE)
    kv = (rms_norm(c_kv, kv_norm) @ w_ukv).reshape(B, L, B_HEADS, B_NOPE + B_V)
    q_nope, q_pe = q[..., :B_NOPE], q[..., B_NOPE:]
    k_nope, v = kv[..., :B_NOPE], kv[..., B_NOPE:]
    cos, sin = rope_tables(L, B_ROPE)
    scale = (B_NOPE + B_ROPE) ** -0.5
    q_nope = q_nope * scale
    q_pe = apply_rope(q_pe, cos[:, None], sin[:, None]) * scale
    k_pe = apply_rope(k_pe, cos, sin)

    causal_m = jnp.tril(jnp.ones((N_META, N_META), dtype=bool))
    s_m = (jnp.einsum('bqhd,bshd->bhqs', q_nope[:, :N_META], k_nope[:, :N_META])
           + jnp.einsum('bqhd,bsd->bhqs', q_pe[:, :N_META], k_pe[:, :N_META])).astype(jnp.float32)
    p_m = jax.nn.softmax(jnp.where(causal_m, s_m, NEG_INF), axis=-1).astype(v.dtype)
    o_m = jnp.einsum('bhqs,bshd->bqhd', p_m, v[:, :N_META]).reshape(B, N_META, B_HEADS * B_V)

    qn_blocks = q_nope[:, N_META:].reshape(B, n_blk, BLOCK, B_HEADS, B_NOPE).transpose(1, 0, 2, 3, 4)
    qp_blocks = q_pe[:, N_META:].reshape(B, n_blk, BLOCK, B_HEADS, B_ROPE).transpose(1, 0, 2, 3, 4)
    k_pos = jnp.arange(L)

    def attend_block(args):
        qn, qp, b = args
        q_pos = N_META + b * BLOCK + jnp.arange(BLOCK)
        s = (jnp.einsum('bqhd,bshd->bhqs', qn, k_nope)
             + jnp.einsum('bqhd,bsd->bhqs', qp, k_pe)).astype(jnp.float32)
        s = jnp.where(k_pos[None, :] <= q_pos[:, None], s, NEG_INF)
        p = jax.nn.softmax(s, axis=-1).astype(v.dtype)
        return jnp.einsum('bhqs,bshd->bqhd', p, v)

    o_r = lax.map(attend_block, (qn_blocks, qp_blocks, jnp.arange(n_blk)))
    o_r = o_r.transpose(1, 0, 2, 3, 4).reshape(B, n_blk * BLOCK, B_HEADS * B_V)
    o = jnp.concatenate([o_m, o_r], axis=1)
    return o @ w_o

def hierarchical_moe(h, w_group, b_group, w_router, b_router, w_gate, w_up, w_down):
    B, L, D = h.shape
    T = B * L
    x = h.reshape(T, D)
    g_prob = jax.nn.softmax((x @ w_group).astype(jnp.float32) + b_group.astype(jnp.float32), axis=-1)
    g_p, g_idx = lax.top_k(g_prob, 1)
    e_logits = ((x @ w_router).astype(jnp.float32) + b_router.astype(jnp.float32)).reshape(T, N_GROUPS, EXPERTS_PER_GROUP)
    e_logits = jnp.take_along_axis(e_logits, g_idx[:, :, None], axis=1)[:, 0]
    e_prob = jax.nn.softmax(e_logits, axis=-1)
    e_p, e_idx = lax.top_k(e_prob, TOP_K)
    weights = g_p * e_p / jnp.sum(e_p, axis=-1, keepdims=True)
    expert_ids = g_idx * EXPERTS_PER_GROUP + e_idx

    n_slots = T * TOP_K
    slot_expert = expert_ids.reshape(-1)
    slot_token = jnp.repeat(jnp.arange(T), TOP_K)
    slot_weight = weights.reshape(-1)
    order = jnp.argsort(slot_expert)
    se, st, sw = slot_expert[order], slot_token[order], slot_weight[order]
    counts = jnp.bincount(slot_expert, length=N_EXPERTS)
    starts = jnp.cumsum(counts) - counts
    padded = (counts + MOE_BLOCK - 1) // MOE_BLOCK * MOE_BLOCK
    pends = jnp.cumsum(padded)
    pstarts = pends - padded
    dest = pstarts[se] + jnp.arange(n_slots) - starts[se]
    n_blocks = -(-(n_slots + N_EXPERTS * (MOE_BLOCK - 1)) // MOE_BLOCK)
    buf = jnp.zeros((n_blocks * MOE_BLOCK, D), x.dtype).at[dest].set(x[st])
    block_expert = jnp.minimum(jnp.searchsorted(pends, jnp.arange(n_blocks) * MOE_BLOCK, side='right'), N_EXPERTS - 1)

    def expert_block(args):
        xb, e = args
        return (jax.nn.silu(xb @ w_gate[e]) * (xb @ w_up[e])) @ w_down[e]

    y_buf = lax.map(expert_block, (buf.reshape(n_blocks, MOE_BLOCK, D), block_expert)).reshape(-1, D)
    y = jax.ops.segment_sum(y_buf[dest] * sw[:, None].astype(y_buf.dtype), st, num_segments=T)
    return y.reshape(B, L, D)

def setup_inputs(seed: int = 0) -> dict:
    key = jax.random.key(seed)
    ks = iter(jax.random.split(key, 32))
    f32 = jnp.float32

    def nrm(shape):
        return jax.random.normal(next(ks), shape, f32)

    def dense(shape, fan_in):
        return nrm(shape) * (fan_in ** -0.5)

    def gain(shape):
        return 1.0 + 0.02 * nrm(shape)

    return {
        "x": nrm((BATCH, SEQ, D_MODEL)),
        "meta_tokens": nrm((N_META, D_MODEL)),
        "attn_norm": gain((DEPTH, D_MODEL)),
        "ffn_norm": gain((DEPTH, D_MODEL)),
        "final_norm": gain((D_MODEL,)),
        "a_w_qkv": dense((N_A_LAYERS, D_MODEL, A_QKV), D_MODEL),
        "a_b_qkv": 0.02 * nrm((N_A_LAYERS, A_QKV)),
        "a_sinks": 0.5 * nrm((N_A_LAYERS, A_HEADS)),
        "a_w_o": dense((N_A_LAYERS, A_Q_W, D_MODEL), A_Q_W),
        "a_b_o": 0.02 * nrm((N_A_LAYERS, D_MODEL)),
        "b_w_in": dense((N_B_LAYERS, D_MODEL, B_IN), D_MODEL),
        "b_q_norm": gain((N_B_LAYERS, B_Q_RANK)),
        "b_kv_norm": gain((N_B_LAYERS, B_KV_RANK)),
        "b_w_uq": dense((N_B_LAYERS, B_Q_RANK, B_HEADS * (B_NOPE + B_ROPE)), B_Q_RANK),
        "b_w_ukv": dense((N_B_LAYERS, B_KV_RANK, B_HEADS * (B_NOPE + B_V)), B_KV_RANK),
        "b_w_o": dense((N_B_LAYERS, B_HEADS * B_V, D_MODEL), B_HEADS * B_V),
        "moe_w_group": dense((DEPTH, D_MODEL, N_GROUPS), D_MODEL),
        "moe_b_group": 0.01 * nrm((DEPTH, N_GROUPS)),
        "moe_w_router": dense((DEPTH, D_MODEL, N_EXPERTS), D_MODEL),
        "moe_b_router": 0.01 * nrm((DEPTH, N_EXPERTS)),
        "moe_w_gate": dense((DEPTH, N_EXPERTS, D_MODEL, D_EXPERT), D_MODEL),
        "moe_w_up": dense((DEPTH, N_EXPERTS, D_MODEL, D_EXPERT), D_MODEL),
        "moe_w_down": dense((DEPTH, N_EXPERTS, D_EXPERT, D_MODEL), D_EXPERT),
    }

def reference(x, meta_tokens, attn_norm, ffn_norm, final_norm,
              a_w_qkv, a_b_qkv, a_sinks, a_w_o, a_b_o,
              b_w_in, b_q_norm, b_kv_norm, b_w_uq, b_w_ukv, b_w_o,
              moe_w_group, moe_b_group, moe_w_router, moe_b_router,
              moe_w_gate, moe_w_up, moe_w_down):
    B = x.shape[0]
    meta = jnp.broadcast_to(meta_tokens[None].astype(x.dtype), (B, N_META, D_MODEL))
    h = jnp.concatenate([meta, x], axis=1)
    for i in range(DEPTH):
        hn = rms_norm(h, attn_norm[i])
        if i % 2 == 0:
            j = i // 2
            mix = swa_sink_attention(hn, a_w_qkv[j], a_b_qkv[j], a_sinks[j], a_w_o[j], a_b_o[j])
        else:
            j = i // 2
            mix = mla_attention(hn, b_w_in[j], b_q_norm[j], b_kv_norm[j], b_w_uq[j], b_w_ukv[j], b_w_o[j])
        h = h + mix
        h = h + hierarchical_moe(rms_norm(h, ffn_norm[i]), moe_w_group[i], moe_b_group[i],
                                 moe_w_router[i], moe_b_router[i],
                                 moe_w_gate[i], moe_w_up[i], moe_w_down[i])
    return rms_norm(h, final_norm)[:, N_META:]


_drawn_inputs = setup_inputs


def setup_inputs(seed=0):
    import zlib

    import numpy as np

    out = dict(_drawn_inputs(seed))
    spreads = {}
    factors = {'final_norm': 2.877,
     'a_sinks': 6.854,
     'b_q_norm': 5.696,
     'b_kv_norm': 6.176,
     'moe_b_group': 3.599}
    for name, (base, spread) in spreads.items():
        noise = np.random.default_rng([zlib.crc32(name.encode()), seed]).standard_normal(out[name].shape)
        drawn = base * np.exp(spread * noise) if base else spread * noise
        out[name] = __import__('jax').numpy.asarray(drawn.astype(out[name].dtype))
    for name, factor in factors.items():
        out[name] = (out[name] * factor).astype(out[name].dtype)
    return out
```

```python
import math
from contextlib import ExitStack

import concourse.bass as bass
import numpy as np
from concourse import mybir

F32 = mybir.dt.float32
F32R = mybir.dt.float32r
BF16 = mybir.dt.bfloat16
I32 = mybir.dt.int32
U32 = mybir.dt.uint32
ALU = mybir.AluOpType
ACT = mybir.ActivationFunctionType
AX = mybir.AxisListType

P = 128
D = 1024
DC = D // P
SEQ = 2048
META = 16
NT = 1 + SEQ // P
ROWS = NT * P
EPS = 1e-6
MASKED = -1e30

HEADS, HD = 16, 64
QW, KVW = HEADS * HD, 2 * HD
QKV = QW + 2 * KVW
BAND = META + 2 * P
A_SCALE = HD ** -0.5

QR, KVR, ROPE = D // 4, D // 8, 32
B_IN = QR + KVR + ROPE
QD = HD + ROPE
B_SCALE = QD ** -0.5
KEYS = META + SEQ

GROUPS, PER, EXPERTS = 4, 8, 32
FE = D // 4
FC = FE // P
CAP = 160
OVER = -(-(KEYS - CAP) // P)
STRIDE = CAP + OVER * P
SLOTS = EXPERTS * STRIDE + 2 * P
TC = [(0, P), (P, CAP - P)]


class At:

    def __init__(self, turn, c, unroll=2):
        self.turn, self.c, self.unroll = turn, c, unroll

    def back(self, k):
        return At(self.turn, self.c - k, self.unroll)

    @property
    def n(self):
        return self.c if self.turn is None else self.turn * self.unroll + self.c

    def live(self, total=NT):
        return self.turn is not None or 0 <= self.c < total

    def after(self, k):
        return self.turn is not None or self.c >= k

    @property
    def slot(self):
        return self.c % 2

    @property
    def uses(self):
        return self.c // 2 if self.turn is None else self.turn * (self.unroll // 2) + self.c // 2

    @property
    def slot4(self):
        return self.c % 4

    @property
    def uses4(self):
        return self.c // 4 if self.turn is None else self.turn + self.c // 4

    def count(self, per, more):
        return self.n * per + more


def over_steps(eng, first, last, loop_from, loop_to, body, unroll=2):
    for c in range(first, loop_from):
        body(At(None, c))
    if loop_to > loop_from:
        with eng.Fori(0, (loop_to - loop_from) // unroll) as turn:
            for k in range(unroll):
                body(At(turn, loop_from + k, unroll))
    for c in range(max(loop_to, loop_from), last):
        body(At(None, c))


class Space:

    def __init__(self, nc, ctx, tag):
        self.nc, self.ctx, self.tag, self.taken = nc, ctx, tag, []
        ctx.callback(self.release)

    def release(self):
        self.nc.clear_and_free_semaphores(self.taken)
        self.nc.all_engine_barrier()

    def sb(self, name, shape, dt=F32):
        return self.ctx.enter_context(self.nc.sbuf_tensor(f"{self.tag}_{name}", shape, dt))

    def ps(self, name, shape, dt=F32):
        return self.ctx.enter_context(self.nc.psum_tensor(f"{self.tag}_{name}", shape, dt))

    def sem(self, name):
        self.taken.append(self.nc.alloc_semaphore(f"{self.tag}_{name}"))
        return self.taken[-1]

    def sems(self, name, k):
        return [self.sem(f"{name}{i}") for i in range(k)]


def rows(t, i):
    if i.turn is None:
        return t[i.c * P:(i.c + 1) * P, :]
    return t[0:t.shape[0] // P * P, :].rearrange("(t p) d -> t p d", p=P)[bass.ds(i.n, 1), :, :].rearrange("a p d -> (a p) d")


def tile_at(i):
    return slice(i.c, i.c + 1) if i.turn is None else bass.ds(i.n, 1)


def bcast(vec, n):
    return vec.rearrange("(a n) -> a n", a=1).to_broadcast([P, n])


def attention_a(nc, io, dram):
    with ExitStack() as ctx:
        s = Space(nc, ctx, "aa")
        NG = 2
        PAIRS = HEADS // 2
        ITEMS = PAIRS + NG
        GI = ITEMS // NG
        GW = [512, 512, QKV - 1024]
        wqkv = s.sb("wqkv", [P, 2, QKV])
        w_hi, w_lo = s.sb("w_hi", [P, DC, QKV], F32R), s.sb("w_lo", [P, DC, QKV], F32R)
        bqkv = s.sb("bqkv", [P, QKV])
        gain = s.sb("gain", [P, D])
        ident = s.sb("ident", [P, P])
        identb = s.sb("identb", [P, P], BF16)
        sinks = s.sb("sinks", [P, HEADS])
        negsinks = s.sb("negsinks", [P, HEADS])
        half = s.sb("half", [P, 1])
        x = s.sb("x", [P, 2, D])
        xsq = s.sb("xsq", [P, D])
        ssq = s.sb("ssq", [P, 2])
        rstd = s.sb("rstd", [P, 2])
        xn = s.sb("xn", [P, D])
        x_hi, x_lo = s.sb("x_hi", [P, DC, P], F32R), s.sb("x_lo", [P, DC, P], F32R)
        cs = s.sb("cs", [P, 2, 2 * HD])
        mask = s.sb("mask", [P, 2, BAND], BF16)
        qkv = s.sb("qkv", [P, QKV])
        qr = s.sb("qr", [P, QW + KVW])
        rot = s.sb("rot", [P, QW + KVW])
        qT = s.sb("qT", [P, 2, DC, P])
        kband = s.sb("kband", [P, 2, BAND])
        kmeta = s.sb("kmeta", [P, META])
        vband = s.sb("vband", [P, 2, 2, KVW])
        vmeta = s.sb("vmeta", [P, NG, 8 * HD])
        prob = s.sb("prob", [P, 2, 8, BAND])
        pmeta = s.sb("pmeta", [P, P])
        pT = s.sb("pT", [P, 2, 4 * P])
        rmax = s.sb("rmax", [P, HEADS])
        negmax = s.sb("negmax", [P, HEADS])
        psum_row = s.sb("psumrow", [P, HEADS])
        den = s.sb("den", [P, 3, HEADS])
        o = s.sb("o", [P, 2, D])
        mm = s.ps("mm", [P, 2, 512])
        S = s.ps("S", [P, 4, 512])
        O = s.ps("O", [P, 2, 512])

        consts = s.sem("consts")
        w_in = s.sems("w_in", 2)
        w_high, w_split = s.sem("w_high"), s.sem("w_split")
        x_split = s.sem("x_split")
        zeroed = s.sem("zeroed")
        held = s.sem("held")
        x_in = s.sems("x_in", 2)
        cs_in = s.sems("cs_in", 2)
        mask_in = s.sems("mask_in", 2)
        squared = s.sem("squared")
        rstd_ready = s.sem("rstd_ready")
        xn_ready = s.sem("xn_ready")
        proj_done = s.sem("proj_done")
        act_copied = s.sem("act_copied")
        added = s.sem("added")
        v_ready = s.sem("v_ready")
        k_ready = s.sem("k_ready")
        roped = s.sem("roped")
        vm_ready = s.sem("vm_ready")
        scored = s.sem("scored")
        maxed = s.sem("maxed")
        exped = s.sem("exped")
        meta_packed = s.sem("meta_packed")
        flipped = s.sem("flipped")
        pT_dve = s.sem("pT_dve")
        pT_act = s.sem("pT_act")
        summed = s.sem("summed")
        sink_in = s.sem("sink_in")
        sink_exped = s.sem("sink_exped")
        o_ready = s.sem("o_ready")
        o_out = s.sems("o_out", 2)

        def item(m):
            g, r = divmod(m, GI)
            return g, (4 * g + r if r < 4 else None)

        def copy_flipped(eng, copy, j, m, done):
            g, p = item(m)
            n = 4 * P if p is not None else P
            eng.wait_ge(flipped, j.count(ITEMS, m + 1))
            if m >= 2 or j.after(1):
                eng.wait_ge(summed, j.count(ITEMS, m - 1))
            copy(pT[:, m % 2, 0:n], mm[:, m % 2, 0:n]).then_inc(done, 1)

        with nc.Block() as block:
            @block.sync
            def _(sp):
                sp.dma_start(gain[:, :], bcast(io["attn_norm"][0, :], D)).then_inc(consts, 16)
                sp.dma_start(ident[:, :], io["ident"]).then_inc(consts, 16)
                sp.dma_start(identb[:, :], io["identb"]).then_inc(consts, 16)
                sp.dma_start(sinks[:, :], bcast(io["a_sinks"][0, :], HEADS)).then_inc(consts, 16)
                sp.dma_start(bqkv[:, :], bcast(io["a_b_qkv"][0, :], QKV)).then_inc(consts, 16)
                for c in range(DC):
                    if c >= 2:
                        sp.wait_ge(w_split, c - 1)
                    sp.dma_start(wqkv[:, c % 2, :], io["a_w_qkv"][0, P * c:P * c + P, :]).then_inc(w_in[c % 2], 16)

                def load_x(i):
                    if i.after(2):
                        sp.wait_ge(xn_ready, i.count(1, -1))
                    if i.turn is None and i.c == 0:
                        sp.wait_ge(zeroed, 1)
                        sp.dma_start(x[0:META, 0, :], io["meta_tokens"]).then_inc(x_in[0], 16)
                    else:
                        sp.dma_start(x[:, i.slot, :], rows(io["x"], i.back(1))).then_inc(x_in[i.slot], 16)

                def load_tables(i):
                    if i.after(2):
                        sp.wait_ge(roped, i.count(1, -1))
                    sp.dma_start(cs[:, i.slot, :], rows(io["cs_a"], i)).then_inc(cs_in[i.slot], 16)

                def step(i):
                    if i.turn is None and i.c == 0:
                        load_x(i)
                        load_x(i.back(-1))
                        load_tables(i)
                    if i.back(-2).live():
                        load_x(i.back(-2))
                    if i.back(-1).live():
                        load_tables(i.back(-1))
                    if i.live():
                        if i.after(2):
                            sp.wait_ge(scored, i.count(PAIRS, -PAIRS))
                        sp.dma_start(mask[:, i.slot, :], rows(io["mask_a"], i)).then_inc(mask_in[i.slot], 16)
                    j = i.back(2)
                    if j.live():
                        sp.wait_ge(o_ready, j.count(2, 2))
                        sp.dma_start(rows(dram["o"], j), o[:, j.slot, :]).then_inc(o_out[j.slot], 16)
                    if i.turn is None and i.c == 0:
                        sp.wait_ge(added, 3)
                        sp.wait_ge(zeroed, 1)
                        for g in range(NG):
                            for h in range(8):
                                sp.dma_start(vmeta[META * h:META * (h + 1), g, HD * h:HD * (h + 1)],
                                             qkv[0:META, QW + KVW + HD * g:QW + KVW + HD * (g + 1)]).then_inc(vm_ready, 16)
                over_steps(sp, 0, 2 + NT, 3, NT - 2, step)
                for b in range(2):
                    sp.wait_ge(o_out[b], 16 * ((NT + 1 - b) // 2))

            @block.gpsimd
            def _(pool):
                nc.gpsimd.memset(x[:, 0, :], 0.0)
                nc.gpsimd.memset(vmeta[:, :, :], 0.0)
                nc.gpsimd.memset(kband[:, :, :], 0.0)
                nc.gpsimd.memset(vband[:, :, :, :], 0.0)
                nc.gpsimd.memset(half[:, :], -0.5)
                pool.wait_ge(consts, 16 * 5)
                nc.gpsimd.tensor_scalar(negsinks[:, :], sinks[:, :], -1.0, None, ALU.mult)
                pool.drain().then_inc(zeroed, 1)

                def norm(i):
                    pool.wait_ge(squared, i.count(1, 1))
                    pool.sem_inc(held, 1)
                    nc.gpsimd.tensor_scalar(rstd[:, i.slot:i.slot + 1], ssq[:, i.slot:i.slot + 1], 1.0 / D, EPS, ALU.mult, ALU.add)
                    pool.drain()
                    nc.gpsimd.tensor_tensor(rstd[:, i.slot:i.slot + 1], rstd[:, i.slot:i.slot + 1], half[:, :], ALU.pow).then_inc(rstd_ready, 1)

                def step(i):
                    if i.back(-1).live():
                        norm(i.back(-1))
                    if i.live():
                        pool.wait_ge(added, i.count(3, 3))
                        if i.after(1):
                            pool.wait_ge(proj_done, i.count(8, 0))
                            if i.after(2):
                                pool.wait_ge(summed, i.back(2).count(ITEMS, ITEMS))
                            pool.sem_inc(held, 1)
                            nc.gpsimd.tensor_copy(vband[:, i.slot, 0, :], vband[:, 1 - i.slot, 1, :])
                        pool.sem_inc(held, 1)
                        nc.gpsimd.tensor_copy(vband[:, i.slot, 1, :], qkv[:, QW + KVW:QKV])
                        pool.wait_ge(cs_in[i.slot], (i.uses + 1) * 16)
                        cos = cs[:, i.slot, 0:HD].unsqueeze(1).to_broadcast([P, 18, HD])
                        nsin = cs[:, i.slot, HD:HD + HD // 2].unsqueeze(1).to_broadcast([P, 18, HD // 2])
                        sin = cs[:, i.slot, HD + HD // 2:2 * HD].unsqueeze(1).to_broadcast([P, 18, HD // 2])
                        qk = qkv[:, 0:QW + KVW].rearrange("p (h d) -> p h d", d=HD)
                        ro = rot[:, :].rearrange("p (h d) -> p h d", d=HD)
                        nc.gpsimd.tensor_tensor(ro[:, :, 0:HD // 2], qk[:, :, HD // 2:HD], nsin, ALU.mult)
                        nc.gpsimd.tensor_tensor(ro[:, :, HD // 2:HD], qk[:, :, 0:HD // 2], sin, ALU.mult)
                        pool.drain()
                        nc.gpsimd.tensor_tensor(qk, qk, cos, ALU.mult)
                        pool.drain()
                        nc.gpsimd.tensor_tensor(qr[:, 0:QW].rearrange("p (h g d) -> p g h d", g=NG, d=HD),
                                                qkv[:, 0:QW].rearrange("p (g h d) -> p g h d", g=NG, d=HD),
                                                rot[:, 0:QW].rearrange("p (g h d) -> p g h d", g=NG, d=HD), ALU.add)
                        nc.gpsimd.tensor_tensor(qr[:, QW:], qkv[:, QW:QW + KVW], rot[:, QW:], ALU.add)
                        pool.drain().then_inc(roped, 1)
                over_steps(pool, -1, NT + 1, 4, NT - 1, step)

            @block.scalar
            def _(act):
                def square(i):
                    if i.after(2):
                        act.wait_ge(xn_ready, i.count(1, -1))
                    act.wait_ge(x_in[i.slot], (i.uses + 1) * 16)
                    if i.turn is None and i.c == 0:
                        act.wait_ge(zeroed, 1)
                    nc.scalar.activation(xsq[:, :], x[:, i.slot, :], ACT.Square, accum_out=ssq[:, i.slot:i.slot + 1])
                    act.drain().then_inc(squared, 1)

                for c in range(DC):
                    act.wait_ge(w_in[c % 2], 16 * (c // 2 + 1))
                    nc.scalar.copy(w_hi[:, c, :], wqkv[:, c % 2, :]).then_inc(w_high, 1)

                def step(i):
                    if i.live():
                        for b in range(2):
                            act.wait_ge(proj_done, i.count(8, 1 + b))
                            nc.scalar.copy(x_hi[:, 4 * b:4 * b + 4, :].rearrange("p c t -> p (c t)"), mm[:, b, :]).then_inc(act_copied, 1)
                    if i.back(-1).live():
                        square(i.back(-1))
                    j = i.back(1)
                    if j.live():
                        for k in range(ITEMS + 2):
                            if k < PAIRS:
                                g = k // 4
                                act.wait_ge(maxed, j.count(PAIRS, k + 1))
                                if k % 4 == 0 and j.after(1):
                                    act.wait_ge(flipped, j.back(1).count(ITEMS, GI * (g + 1)))
                                for h in (2 * k, 2 * k + 1):
                                    last = nc.scalar.activation(prob[:, g, h % 8, :], S[:, h % 4, 0:BAND], ACT.Exp, bias=negmax[:, h:h + 1],
                                                                scale=A_SCALE, accum_out=psum_row[:, h:h + 1])
                                last.then_inc(exped, 1)
                                if k % 4 == 3:
                                    act.drain()
                                    if g == 1 or j.after(1):
                                        act.wait_ge(flipped, j.count(ITEMS, GI * g))
                                    nc.scalar.copy(pmeta[:, :].rearrange("p (h k) -> p h k", k=META), prob[:, g, :, 0:META]).then_inc(meta_packed, 1)
                            if k >= 2 and k % 2:
                                copy_flipped(act, nc.scalar.copy, j, k - 2, pT_act)
                            if k in (4, 8):
                                g = k // 4 - 1
                                act.wait_ge(sink_in, j.count(2, g + 1))
                                nc.scalar.activation(den[:, 1, 8 * g:8 * g + 8], den[:, 0, 8 * g:8 * g + 8], ACT.Exp).then_inc(sink_exped, 1)
                    if i.live():
                        for b in range(2):
                            act.wait_ge(proj_done, i.count(8, 6 + b))
                            nc.scalar.copy(qT[:, i.slot, 4 * b:4 * b + 4, :].rearrange("p c t -> p (c t)"), mm[:, 1 - b, :]).then_inc(act_copied, 1)
                        act.wait_ge(proj_done, i.count(8, 8))
                        if i.turn is None and i.c == 0:
                            act.wait_ge(zeroed, 1)
                            nc.scalar.copy(kmeta[:, :], mm[:, 1, 0:META])
                        else:
                            nc.scalar.copy(kband[:, i.slot, META:META + P], kband[:, 1 - i.slot, META + P:BAND])
                            nc.scalar.copy(kband[:, i.slot, 0:META], kmeta[:, :])
                        nc.scalar.copy(kband[:, i.slot, META + P:BAND], mm[:, 1, 0:P]).then_inc(act_copied, 1)
                        act.drain().then_inc(k_ready, 1)
                over_steps(act, -1, NT + 1, 4, NT - 1, step)

            @block.vector
            def _(dve):
                dve.wait_ge(consts, 16 * 5)
                dve.wait_ge(zeroed, 1)

                def low_part(low, whole, high):
                    return nc.vector.tensor_tensor(low, whole, high.bitcast(F32), ALU.subtract)

                for c in range(DC):
                    dve.wait_ge(w_high, c + 1)
                    low_part(w_lo[:, c, :], wqkv[:, c % 2, :], w_hi[:, c, :]).then_inc(w_split, 1)

                def normalise(i):
                    dve.wait_ge(rstd_ready, i.count(1, 1))
                    if i.after(1):
                        dve.wait_ge(proj_done, i.back(1).count(8, 2))
                    nc.vector.scalar_tensor_tensor(out=xn[:, :], in0=x[:, i.slot, :], scalar=rstd[:, i.slot:i.slot + 1],
                                                   in1=gain[:, :], op0=ALU.mult, op1=ALU.mult).then_inc(xn_ready, 1)

                def step(i):
                    if i.live():
                        for b in range(2):
                            dve.wait_ge(act_copied, i.count(5, 1 + b))
                            low_part(x_lo[:, 4 * b:4 * b + 4, :].rearrange("p c t -> p (c t)"), mm[:, b, :],
                                     x_hi[:, 4 * b:4 * b + 4, :].rearrange("p c t -> p (c t)")).then_inc(x_split, 1)
                    if i.back(-1).live():
                        normalise(i.back(-1))
                    if i.live():
                        if i.after(1):
                            dve.wait_ge(roped, i.count(1, 0))
                        if i.turn is None and i.c == 1:
                            dve.wait_ge(vm_ready, 16 * 16)
                        for g in range(3):
                            dve.wait_ge(proj_done, i.count(8, 3 + g))
                            nc.vector.tensor_tensor(qkv[:, 512 * g:512 * g + GW[g]], mm[:, g % 2, 0:GW[g]],
                                                    bqkv[:, 512 * g:512 * g + GW[g]], ALU.add).then_inc(added, 1)
                    j = i.back(1)
                    if j.live():
                        for k in range(ITEMS + 3):
                            if k < PAIRS:
                                hs = slice(2 * k, 2 * k + 2)
                                dve.wait_ge(scored, j.count(PAIRS, k + 1))
                                if j.after(1):
                                    dve.wait_ge(exped, j.back(1).count(PAIRS, k + 1))
                                nc.vector.reduce_max(rmax[:, hs], S[:, 2 * (k % 2):2 * (k % 2) + 2, 0:BAND], AX.X)
                                dve.drain()
                                nc.vector.scalar_tensor_tensor(out=negmax[:, hs], in0=rmax[:, hs], scalar=-A_SCALE, in1=negsinks[:, hs],
                                                               op0=ALU.mult, op1=ALU.min).then_inc(maxed, 1)
                                if k % 4 == 3:
                                    g = k // 4
                                    dve.drain()
                                    nc.vector.tensor_tensor(den[:, 0, 8 * g:8 * g + 8], sinks[:, 8 * g:8 * g + 8],
                                                            negmax[:, 8 * g:8 * g + 8], ALU.add).then_inc(sink_in, 1)
                            if 2 <= k < ITEMS + 2 and k % 2 == 0:
                                copy_flipped(dve, nc.vector.tensor_copy, j, k - 2, pT_dve)
                            if k in (8, 12):
                                g = k // 4 - 2
                                dve.wait_ge(sink_exped, j.count(2, g + 1))
                                dve.wait_ge(exped, j.count(PAIRS, 4 * (g + 1)))
                                nc.vector.tensor_tensor(den[:, 2, 8 * g:8 * g + 8], den[:, 1, 8 * g:8 * g + 8],
                                                        psum_row[:, 8 * g:8 * g + 8], ALU.add)
                                dve.drain()
                                nc.vector.reciprocal(den[:, 2, 8 * g:8 * g + 8], den[:, 2, 8 * g:8 * g + 8])
                                dve.drain()
                                dve.wait_ge(summed, j.count(ITEMS, GI * (g + 1)))
                                if j.after(2):
                                    dve.wait_ge(o_out[j.slot], j.uses * 16)
                                nc.vector.tensor_tensor(
                                    o[:, j.slot, 512 * g:512 * g + 512].rearrange("p (h d) -> p h d", d=HD),
                                    O[:, g, :].rearrange("p (h d) -> p h d", d=HD),
                                    den[:, 2, 8 * g:8 * g + 8].unsqueeze(2).to_broadcast([P, 8, HD]), ALU.mult).then_inc(o_ready, 1)
                over_steps(dve, -1, NT + 1, 4, NT - 1, step)

            @block.tensor
            def _(pe):
                pe.wait_ge(consts, 16 * 5)
                pe.wait_ge(w_split, DC)

                def step(i):
                    if i.live():
                        pe.wait_ge(xn_ready, i.count(1, 1))
                        for b in range(2):
                            if i.after(1):
                                pe.wait_ge(act_copied, i.count(5, -1 + b))
                            for c in range(4 * b, 4 * b + 4):
                                last = nc.tensor.transpose(mm[:, b, P * (c % 4):P * (c % 4) + P], xn[:, P * c:P * c + P], ident[:, :])
                            last.then_inc(proj_done, 1)
                        for g in range(3):
                            pe.wait_ge(x_split, i.count(2, 2))
                            if g == 2:
                                pe.wait_ge(added, i.count(3, 1))
                            for c in range(DC):
                                to, w = mm[:, g % 2, 0:GW[g]], slice(512 * g, 512 * g + GW[g])
                                nc.tensor.matmul(to, x_hi[:, c, :], w_hi[:, c, w], start=(c == 0), stop=False)
                                nc.tensor.matmul(to, x_hi[:, c, :], w_lo[:, c, w], start=False, stop=False)
                                last = nc.tensor.matmul(to, x_lo[:, c, :], w_hi[:, c, w], start=False, stop=(c == DC - 1))
                            last.then_inc(proj_done, 1)
                    j = i.back(1)
                    if j.live():
                        pe.wait_ge(k_ready, j.count(1, 1))
                        pe.wait_ge(roped, j.count(1, 1))
                        pe.wait_ge(mask_in[j.slot], (j.uses + 1) * 16)
                        if j.turn is None and j.c == 0:
                            pe.wait_ge(vm_ready, 16 * 16)
                        for k in range(ITEMS + 3):
                            if k < PAIRS:
                                lo = (k // 4) * HD
                                if k >= 2 or j.after(1):
                                    pe.wait_ge(exped, j.count(PAIRS, k - 1))
                                for h in (2 * k, 2 * k + 1):
                                    nc.tensor.matmul(S[:, h % 4, 0:BAND], qT[lo:lo + HD, j.slot, h % 8, :], kband[lo:lo + HD, j.slot, :],
                                                     start=True, stop=False)
                                    last = nc.tensor.matmul(S[:, h % 4, 0:BAND], identb[:, :], mask[:, j.slot, :], start=False, stop=True)
                                last.then_inc(scored, 1)
                            if 2 <= k < ITEMS + 2:
                                m = k - 2
                                g, p = item(m)
                                pe.wait_ge(exped, j.count(PAIRS, (p if p is not None else 4 * g + 3) + 1))
                                if m >= 2:
                                    pe.wait_ge((pT_dve, pT_act)[m % 2], j.count(ITEMS // 2, m // 2))
                                elif i.live():
                                    pe.wait_ge(added, i.count(3, 3 - m))
                                if p is None:
                                    pe.wait_ge(meta_packed, j.count(2, g + 1))
                                    last = nc.tensor.transpose(mm[:, m % 2, 0:P], pmeta[:, :], ident[:, :])
                                else:
                                    for a in range(4):
                                        h, b = 2 * p + a // 2, a % 2
                                        last = nc.tensor.transpose(mm[:, m % 2, P * a:P * a + P],
                                                                   prob[:, g, h % 8, META + P * b:META + P * b + P], ident[:, :])
                                last.then_inc(flipped, 1)
                            if k >= 3:
                                m = k - 3
                                g, p = item(m)
                                pe.wait_ge((pT_dve, pT_act)[m % 2], j.count(ITEMS // 2, m // 2 + 1))
                                if m % GI == 0 and j.after(1):
                                    pe.wait_ge(o_ready, j.back(1).count(2, g + 1))
                                if p is None:
                                    last = nc.tensor.matmul(O[:, g, :], pT[:, m % 2, 0:P], vmeta[:, g, :], start=False, stop=True, skip_group_check=True)
                                else:
                                    for a in range(4):
                                        h, b = 2 * p + a // 2, a % 2
                                        last = nc.tensor.matmul(O[:, g, HD * (h % 8):HD * (h % 8) + HD], pT[:, m % 2, P * a:P * a + P],
                                                                vband[:, j.slot, b, HD * g:HD * g + HD],
                                                                start=(h % 8 == 0 and b == 0), stop=False, skip_group_check=True)
                                last.then_inc(summed, 1)
                    if i.live():
                        pe.wait_ge(roped, i.count(1, 1))
                        for b in range(2):
                            if j.live():
                                pe.wait_ge((pT_act, pT_dve)[b], j.count(ITEMS // 2, ITEMS // 2))
                            for c in range(4 * b, 4 * b + 4):
                                last = nc.tensor.transpose(mm[:, 1 - b, P * (c % 4):P * (c % 4) + P],
                                                           qr[:, P * c:P * c + P], ident[:, :])
                            last.then_inc(proj_done, 1)
                        pe.wait_ge(act_copied, i.count(5, 3))
                        nc.tensor.transpose(mm[:, 1, 0:P], qr[:, QW:QW + KVW], ident[:, :]).then_inc(proj_done, 1)
                over_steps(pe, 0, NT + 1, 4, NT - 1, step)


def project_and_route(nc, io, dram, keep, layer):
    with ExitStack() as ctx:
        s = Space(nc, ctx, f"pr{layer}")
        first = layer == 0
        NL = GROUPS + EXPERTS
        wo = s.sb("wo", [P, 4, D])
        wo_hi, wo_lo = s.sb("wo_hi", [P, DC, D], F32R), s.sb("wo_lo", [P, DC, D], F32R)
        wr = s.sb("wr", [P, DC, NL])
        br = s.sb("br", [P, NL])
        bo = s.sb("bo", [P, D])
        gain = s.sb("gain", [P, D])
        ident = s.sb("ident", [P, P])
        half = s.sb("half", [P, 1])
        iota = s.sb("iota", [P, EXPERTS])
        base = s.sb("base", [P, EXPERTS])
        tri = s.sb("tri", [P, 2 * P], BF16)
        zero = s.sb("zero", [P, D])
        free = s.sb("free", [P, SLOTS // P, 2], I32)
        o = s.sb("o", [P, 2, D])
        res = s.sb("res", [P, 2, D])
        info = s.sb("info", [P, NT, 7])
        h = s.sb("h", [P, 2, D])
        hsq = s.sb("hsq", [P, D])
        ssq = s.sb("ssq", [P, 2])
        rstd = s.sb("rstd", [P, 2])
        xn = s.sb("xn", [P, 2, D])
        o_hi, o_lo = s.sb("o_hi", [P, DC, P], F32R), s.sb("o_lo", [P, DC, P], F32R)
        xT = s.sb("xT", [P, DC, P])
        lg = s.sb("lg", [P, 8 + EXPERTS])
        gmax = s.sb("gmax", [P, 8])
        gidx = s.sb("gidx", [P, 8], U32)
        gneg = s.sb("gneg", [P, 1])
        gexp = s.sb("gexp", [P, GROUPS])
        gsum = s.sb("gsum", [P, 1])
        gid = s.sb("gid", [P, 2])
        ghot = s.sb("ghot", [P, GROUPS])
        picked = s.sb("picked", [P, GROUPS, PER])
        el = s.sb("el", [P, PER])
        emax = s.sb("emax", [P, 8])
        eidx = s.sb("eidx", [P, 8], U32)
        eneg = s.sb("eneg", [P, 1])
        eexp = s.sb("eexp", [P, 2])
        esum = s.sb("esum", [P, 1])
        eid = s.sb("eid", [P, 2])
        hot = s.sb("hot", [P, 2, 2, EXPERTS])
        both = s.sb("both", [P, 2, EXPERTS], BF16)
        run = s.sb("run", [P, EXPERTS])
        place = s.sb("place", [P, EXPERTS])
        junk = s.sb("junk", [P, EXPERTS])
        dest = s.sb("dest", [P, 2])
        desti = s.sb("desti", [P, 2, 2], I32)
        rowi = s.sb("rowi", [P, 2, 2, 2], I32)
        cnt = s.sb("cnt", [P, EXPERTS + 1])
        TO = s.ps("TO", [P, 2, 512])
        PR = s.ps("PR", [P, 2, 512])
        TX = s.ps("TX", [P, 2, 512])
        LG = s.ps("LG", [P, 512])
        RK = s.ps("RK", [P, 512])

        consts = s.sem("consts")
        NCONST = 9 if first else 8
        w_in = s.sems("w_in", 4)
        w_high, w_split = s.sem("w_high"), s.sem("w_split")
        NCLEAR = 4 if first else 1
        zeroed = s.sem("zeroed")
        cleared = s.sem("cleared")
        held = s.sem("held")
        o_in = s.sems("o_in", 2)
        res_in = s.sems("res_in", 2)
        biased = s.sem("biased")
        flipped_o = s.sem("flipped_o")
        o_high = s.sem("o_high")
        o_split = s.sem("o_split")
        projected = s.sem("projected")
        h_ready = s.sem("h_ready")
        squared = s.sem("squared")
        rstd_ready = s.sem("rstd_ready")
        xn_ready = s.sem("xn_ready")
        flipped_x = s.sem("flipped_x")
        copied_x = s.sem("copied_x")
        scored = s.sem("scored")
        logits = s.sem("logits")
        gexped = s.sem("gexped")
        emaxed = s.sem("emaxed")
        eexped = s.sem("eexped")
        chosen = s.sem("chosen")
        weighed = s.sem("weighed")
        ranked = s.sem("ranked")
        placed = s.sem("placed")
        scattered = s.sems("scattered", 2)
        h_out = s.sems("h_out", 2)
        xn_out = s.sems("xn_out", 2)

        with nc.Block() as block:
            @block.sync
            def _(sp):
                sp.dma_start(gain[:, :], bcast(io["ffn_norm"][layer, :], D)).then_inc(consts, 16)
                sp.dma_start(ident[:, :], io["ident"]).then_inc(consts, 16)
                sp.dma_start(iota[:, :], io["iota"]).then_inc(consts, 16)
                sp.dma_start(info[:, :, :], io["info"].rearrange("(t p) a -> p t a", p=P)).then_inc(consts, 16)
                sp.dma_start(base[:, :], io["base"]).then_inc(consts, 16)
                sp.dma_start(tri[:, :], io["ones_tri"]).then_inc(consts, 16)
                sp.dma_start(wr[:, :, 0:GROUPS], io["moe_w_group"][layer, :, :].rearrange("(c p) n -> p c n", p=P)).then_inc(consts, 16)
                sp.dma_start(wr[:, :, GROUPS:NL], io["moe_w_router"][layer, :, :].rearrange("(c p) n -> p c n", p=P)).then_inc(consts, 16)
                wo_dram = (io["a_w_o"] if first else io["b_w_o"])[0, :, :].rearrange("(c p) n -> p c n", p=P)
                for c in range(DC):
                    if c >= 4:
                        sp.wait_ge(w_split, c - 3)
                    sp.dma_start(wo[:, c % 4, :], wo_dram[:, c, :]).then_inc(w_in[c % 4], 16)
                sp.wait_ge(zeroed, 1)
                sp.dma_start(dram["slot"].rearrange("(p n) a -> p n a", p=P), free[:, :, :]).then_inc(cleared, 16)
                if first:
                    sp.dma_start(bo[:, :], bcast(io["a_b_o"][0, :], D)).then_inc(consts, 16)
                    sp.dma_start(dram["xn"][ROWS:ROWS + P, :], zero[:, :]).then_inc(cleared, 16)
                    for k in range(2):
                        sp.dma_start(dram["y"][P * k:P * k + P, :], zero[:, :]).then_inc(cleared, 16)
                sp.dma_start(br[:, 0:GROUPS], bcast(io["moe_b_group"][layer, :], GROUPS)).then_inc(keep["bias_in"], 16)
                sp.dma_start(br[:, GROUPS:NL], bcast(io["moe_b_router"][layer, :], EXPERTS)).then_inc(keep["bias_in"], 16)

                def load(i):
                    if i.after(2):
                        sp.wait_ge(flipped_o, i.back(2).count(2, 2))
                    sp.dma_start(o[:, i.slot, :], rows(dram["o"], i)).then_inc(o_in[i.slot], 16)
                    if i.after(2):
                        sp.wait_ge(h_ready, i.back(2).count(2, 2))
                    if not first:
                        sp.dma_start(res[:, i.slot, :], rows(dram["h"], i)).then_inc(res_in[i.slot], 16)
                    elif i.turn is None and i.c == 0:
                        sp.dma_start(res[0:META, 0, :], io["meta_tokens"]).then_inc(res_in[0], 16)
                    else:
                        sp.dma_start(res[:, i.slot, :], rows(io["x"], i.back(1))).then_inc(res_in[i.slot], 16)

                def step(i):
                    if i.turn is None and i.c == 0:
                        load(i)
                    j = i.back(1)
                    if i.back(-1).live():
                        load(i.back(-1))
                    if j.live():
                        sp.wait_ge(h_ready, j.count(2, 2))
                        sp.dma_start(rows(dram["h"], j), h[:, j.slot, :]).then_inc(h_out[j.slot], 16)
                        sp.wait_ge(xn_ready, j.count(1, 1))
                        sp.dma_start(rows(dram["xn"], j), xn[:, j.slot, :]).then_inc(xn_out[j.slot], 16)
                over_steps(sp, 0, 1 + NT, 4, NT - 1, step)
                for b in range(2):
                    sp.wait_ge(h_out[b], 16 * ((NT + 1 - b) // 2))
                    sp.wait_ge(xn_out[b], 16 * ((NT + 1 - b) // 2))

            @block.gpsimd
            def _(pool):
                nc.gpsimd.memset(half[:, :], -0.5)
                nc.gpsimd.memset(zero[:, :], 0.0)
                nc.gpsimd.memset(free[:, :, 0], ROWS)
                nc.gpsimd.memset(free[:, :, 1], 2 * ROWS)
                nc.gpsimd.memset(res[:, 0, :], 0.0)
                nc.gpsimd.memset(lg[:, :], -3e38)
                pool.drain().then_inc(zeroed, 1)
                pool.wait_ge(zeroed, 1)
                pool.wait_ge(consts, 16 * NCONST)
                nc.gpsimd.tensor_copy(run[:, :], base[:, :])
                pool.drain().then_inc(zeroed, 1)
                pool.wait_ge(cleared, 16 * NCLEAR)

                def bias(i):
                    pool.wait_ge(res_in[i.slot], (i.uses + 1) * 16)
                    nc.gpsimd.tensor_tensor(res[:, i.slot, :], res[:, i.slot, :], bo[:, :], ALU.add).then_inc(biased, 1)

                def step(i):
                    if i.turn is None and i.c == 0 and first:
                        bias(i)
                    if i.live():
                        pool.wait_ge(squared, i.count(1, 1))
                        pool.sem_inc(held, 1)
                        nc.gpsimd.tensor_scalar(rstd[:, i.slot:i.slot + 1], ssq[:, i.slot:i.slot + 1], 1.0 / D, EPS, ALU.mult, ALU.add)
                        pool.drain()
                        nc.gpsimd.tensor_tensor(rstd[:, i.slot:i.slot + 1], rstd[:, i.slot:i.slot + 1], half[:, :], ALU.pow).then_inc(rstd_ready, 1)
                    if i.back(-1).live() and first:
                        bias(i.back(-1))
                    j = i.back(2)
                    if j.live():
                        pool.wait_ge(placed, j.count(1, 1))
                        pool.sem_inc(held, 1)
                        for k in range(2):
                            pool.indirect_dma_start(dram["slot"], bass.IndirectOffsetOnAxis(ap=desti[:, j.slot, k:k + 1], axis=0),
                                                    rowi[:, j.slot, k, :], None).then_inc(scattered[j.slot], 16)
                over_steps(pool, 0, 2 + NT, 4, NT - 1, step)
                for b in range(2):
                    pool.wait_ge(scattered[b], 32 * ((NT + 1 - b) // 2))

            @block.scalar
            def _(act):
                for c in range(DC):
                    act.wait_ge(w_in[c % 4], 16 * (c // 4 + 1))
                    nc.scalar.copy(wo_hi[:, c, :], wo[:, c % 4, :]).then_inc(w_high, 1)
                act.wait_ge(consts, 16 * NCONST)

                def step(i):
                    n = i.back(-1)
                    if n.live():
                        for b in range(2):
                            act.wait_ge(flipped_o, n.count(2, 1 + b))
                            if n.after(1):
                                act.wait_ge(projected, i.count(2, 2))
                            nc.scalar.copy(o_hi[:, 4 * b:4 * b + 4, :].rearrange("p c t -> p (c t)"), TO[:, b, :]).then_inc(o_high, 1)
                    j = i.back(1)
                    if j.live():
                        for b in range(2):
                            act.wait_ge(flipped_x, j.count(2, 1 + b))
                            nc.scalar.copy(xT[:, 4 * b:4 * b + 4, :].rearrange("p c t -> p (c t)"), TX[:, b, :]).then_inc(copied_x, 1)
                    if i.live():
                        act.wait_ge(h_ready, i.count(2, 2))
                        nc.scalar.activation(hsq[:, :], h[:, i.slot, :], ACT.Square, accum_out=ssq[:, i.slot:i.slot + 1])
                        act.drain().then_inc(squared, 1)
                    if j.live():
                        act.wait_ge(logits, j.count(1, 1))
                        nc.scalar.activation(gexp[:, :], lg[:, 0:GROUPS], ACT.Exp, bias=gneg[:, :], accum_out=gsum[:, :])
                        act.drain().then_inc(gexped, 1)
                        act.wait_ge(emaxed, j.count(1, 1))
                        nc.scalar.activation(eexp[:, :], emax[:, 0:2], ACT.Exp, bias=eneg[:, :], accum_out=esum[:, :])
                        act.drain().then_inc(eexped, 1)
                over_steps(act, -1, 1 + NT, 4, NT - 1, step)

            @block.vector
            def _(dve):
                def low_part(low, whole, high):
                    return nc.vector.tensor_tensor(low, whole, high.bitcast(F32), ALU.subtract)

                for c in range(DC):
                    dve.wait_ge(w_high, c + 1)
                    low_part(wo_lo[:, c, :], wo[:, c % 4, :], wo_hi[:, c, :]).then_inc(w_split, 1)
                dve.wait_ge(consts, 16 * NCONST)
                dve.wait_ge(keep["bias_in"], 32 * (layer + 1))
                dve.wait_ge(zeroed, 2)

                def route(j):
                    dve.wait_ge(scored, j.count(1, 1))
                    nc.vector.tensor_tensor(lg[:, 0:GROUPS], LG[:, 0:GROUPS], br[:, 0:GROUPS], ALU.add)
                    nc.vector.tensor_tensor(lg[:, 8:8 + EXPERTS], LG[:, GROUPS:NL], br[:, GROUPS:NL], ALU.add)
                    dve.drain()
                    nc.vector.max(gmax[:, :], lg[:, 0:8])
                    dve.drain()
                    nc.vector.tensor_scalar(gneg[:, :], gmax[:, 0:1], -1.0, None, ALU.mult)
                    dve.drain().then_inc(logits, 1)
                    nc.vector.max_index(gidx[:, :], gmax[:, :], lg[:, 0:8])
                    dve.drain()
                    nc.vector.tensor_copy(gid[:, 0:1], gidx[:, 0:1])
                    dve.drain()
                    nc.vector.tensor_scalar(gid[:, 1:2], gid[:, 0:1], float(PER), None, ALU.mult)
                    nc.vector.tensor_scalar(ghot[:, :], iota[:, 0:GROUPS], gid[:, 0:1], None, ALU.is_equal)
                    dve.drain()
                    nc.vector.tensor_tensor(picked[:, :, :], lg[:, 8:8 + EXPERTS].rearrange("p (g e) -> p g e", e=PER),
                                            ghot[:, :].unsqueeze(2).to_broadcast([P, GROUPS, PER]), ALU.mult)
                    dve.drain()
                    nc.vector.reduce_sum(el[:, :], picked[:, :, :].rearrange("p g e -> p e g"), AX.X)
                    dve.drain()
                    nc.vector.max(emax[:, :], el[:, :])
                    dve.drain()
                    nc.vector.tensor_scalar(eneg[:, :], emax[:, 0:1], -1.0, None, ALU.mult)
                    dve.drain().then_inc(emaxed, 1)
                    nc.vector.max_index(eidx[:, :], emax[:, :], el[:, :])
                    dve.drain()
                    nc.vector.tensor_copy(eid[:, :], eidx[:, 0:2])
                    dve.drain()
                    nc.vector.tensor_scalar(eid[:, :], eid[:, :], gid[:, 1:2], None, ALU.add)
                    dve.drain()
                    about = info[:, tile_at(j), :].rearrange("p a k -> p (a k)")
                    for k in range(2):
                        nc.vector.tensor_scalar(hot[:, j.slot, k, :], iota[:, :], eid[:, k:k + 1], about[:, 0:1],
                                                ALU.is_equal, ALU.mult)
                    dve.drain()
                    nc.vector.tensor_tensor(both[:, j.slot, :], hot[:, j.slot, 0, :], hot[:, j.slot, 1, :], ALU.add).then_inc(chosen, 1)
                    dve.wait_ge(gexped, j.count(1, 1))
                    dve.wait_ge(eexped, j.count(1, 1))
                    nc.vector.tensor_tensor(esum[:, :], esum[:, :], gsum[:, :], ALU.mult)
                    dve.drain()
                    nc.vector.reciprocal(esum[:, :], esum[:, :])
                    dve.drain()
                    nc.vector.tensor_scalar(keep["weights"][:, tile_at(j), :].rearrange("p a k -> p (a k)"), eexp[:, :], esum[:, :], None, ALU.mult)
                    dve.drain().then_inc(weighed, 1)

                def place_tile(j):
                    dve.wait_ge(ranked, j.count(1, 1))
                    if j.after(2):
                        dve.wait_ge(scattered[j.slot], j.uses * 32)
                    about = info[:, tile_at(j), :].rearrange("p a k -> p (a k)")
                    nc.vector.tensor_tensor(place[:, :], RK[:, 0:EXPERTS], run[:, :], ALU.add)
                    nc.vector.tensor_copy(rowi[:, j.slot, :, :].rearrange("p k a -> p (k a)"), about[:, 3:7])
                    dve.drain()
                    for k in range(2):
                        nc.vector.tensor_tensor_reduce(out=junk[:, :], in0=hot[:, j.slot, k, :], in1=place[:, :], scale=1.0, scalar=0.0,
                                                       op0=ALU.mult, op1=ALU.add, accum_out=dest[:, k:k + 1])
                        dve.drain()
                    nc.vector.tensor_tensor(run[:, :], run[:, :], RK[:, EXPERTS:2 * EXPERTS], ALU.add)
                    nc.vector.tensor_tensor(desti[:, j.slot, :], dest[:, :], about[:, 1:3], ALU.add)
                    dve.drain()
                    dve.drain().then_inc(placed, 1)

                def step(i):
                    if i.live():
                        for b in range(2):
                            dve.wait_ge(projected, i.count(2, 1 + b))
                            if b == 0:
                                if first:
                                    dve.wait_ge(biased, i.count(1, 1))
                                else:
                                    dve.wait_ge(res_in[i.slot], (i.uses + 1) * 16)
                                if i.after(2):
                                    dve.wait_ge(h_out[i.slot], i.uses * 16)
                            nc.vector.tensor_tensor(h[:, i.slot, 512 * b:512 * b + 512], PR[:, b, :], res[:, i.slot, 512 * b:512 * b + 512],
                                                    ALU.add).then_inc(h_ready, 1)
                    n = i.back(-1)
                    if n.live():
                        for b in range(2):
                            dve.wait_ge(o_high, n.count(2, 1 + b))
                            low_part(o_lo[:, 4 * b:4 * b + 4, :].rearrange("p c t -> p (c t)"), TO[:, b, :],
                                     o_hi[:, 4 * b:4 * b + 4, :].rearrange("p c t -> p (c t)")).then_inc(o_split, 1)
                    j = i.back(1)
                    if j.live():
                        route(j)
                    if i.live():
                        dve.wait_ge(rstd_ready, i.count(1, 1))
                        dve.wait_ge(h_ready, i.count(2, 2))
                        if i.after(2):
                            dve.wait_ge(xn_out[i.slot], i.uses * 16)
                        nc.vector.scalar_tensor_tensor(out=xn[:, i.slot, :], in0=h[:, i.slot, :], scalar=rstd[:, i.slot:i.slot + 1],
                                                       in1=gain[:, :], op0=ALU.mult, op1=ALU.mult).then_inc(xn_ready, 1)
                    if i.back(2).live():
                        place_tile(i.back(2))
                over_steps(dve, -1, 2 + NT, 4, NT - 1, step)
                nc.vector.tensor_tensor(cnt[:, 0:EXPERTS], run[:, :], base[:, :], ALU.subtract)
                dve.drain()
                nc.vector.tensor_scalar(junk[:, :], cnt[:, 0:EXPERTS], -float(CAP), 0.0, ALU.add, ALU.max)
                dve.drain()
                nc.vector.reduce_sum(cnt[:, EXPERTS:EXPERTS + 1], junk[:, :], AX.X)
                dve.drain()
                nc.vector.tensor_copy(keep["counts"][:, :], cnt[:, :])
                dve.drain()

            @block.tensor
            def _(pe):
                pe.wait_ge(consts, 16 * NCONST)
                pe.wait_ge(w_split, DC)

                def step(i):
                    if i.live():
                        for b in range(2):
                            pe.wait_ge(o_split, i.count(2, 2))
                            if i.after(1):
                                pe.wait_ge(h_ready, i.back(1).count(2, 1 + b))
                            for c in range(DC):
                                w = slice(512 * b, 512 * b + 512)
                                nc.tensor.matmul(PR[:, b, :], o_hi[:, c, :], wo_hi[:, c, w], start=(c == 0), stop=False)
                                nc.tensor.matmul(PR[:, b, :], o_hi[:, c, :], wo_lo[:, c, w], start=False, stop=False)
                                last = nc.tensor.matmul(PR[:, b, :], o_lo[:, c, :], wo_hi[:, c, w], start=False, stop=(c == DC - 1))
                            last.then_inc(projected, 1)
                    k = i.back(2)
                    if k.live():
                        pe.wait_ge(chosen, k.count(1, 1))
                        if k.after(1):
                            pe.wait_ge(placed, k.count(1, 0))
                        nc.tensor.matmul(RK[:, 0:EXPERTS], tri[:, 0:P], both[:, k.slot, :], start=True, stop=True)
                        nc.tensor.matmul(RK[:, EXPERTS:2 * EXPERTS], tri[:, P:2 * P], both[:, k.slot, :], start=True, stop=True).then_inc(ranked, 1)
                    n = i.back(-1)
                    if n.live():
                        pe.wait_ge(o_in[n.slot], (n.uses + 1) * 16)
                        for b in range(2):
                            if n.after(1):
                                pe.wait_ge(o_split, i.count(2, 1 + b))
                            for c in range(4 * b, 4 * b + 4):
                                last = nc.tensor.transpose(TO[:, b, P * (c % 4):P * (c % 4) + P], o[:, n.slot, P * c:P * c + P], ident[:, :])
                            last.then_inc(flipped_o, 1)
                    j = i.back(1)
                    if j.live():
                        pe.wait_ge(xn_ready, j.count(1, 1))
                        for b in range(2):
                            if j.after(1):
                                pe.wait_ge(copied_x, j.back(1).count(2, 1 + b))
                            for c in range(4 * b, 4 * b + 4):
                                last = nc.tensor.transpose(TX[:, b, P * (c % 4):P * (c % 4) + P], xn[:, j.slot, P * c:P * c + P], ident[:, :])
                            last.then_inc(flipped_x, 1)
                        pe.wait_ge(copied_x, j.count(2, 2))
                        if j.after(1):
                            pe.wait_ge(emaxed, j.count(1, 0))
                        for c in range(DC):
                            last = nc.tensor.matmul(LG[:, 0:NL], xT[:, c, :], wr[:, c, :], start=(c == 0), stop=(c == DC - 1))
                        last.then_inc(scored, 1)
                over_steps(pe, -1, 2 + NT, 4, NT - 1, step)


def experts(nc, io, dram, keep, layer):
    with ExitStack() as ctx:
        s = Space(nc, ctx, f"ex{layer}")
        XB = [(0, 3), (3, 6), (6, 8)]
        ident = s.sb("ident", [P, P])
        wg = s.sb("wg", [P, 2, DC, FE])
        wu = s.sb("wu", [P, 2, DC, FE])
        wd = s.sb("wd", [P, 2, FC * D])
        wd_hi, wd_lo = s.sb("wd_hi", [P, FC, D], F32R), s.sb("wd_lo", [P, FC, D], F32R)
        slot = s.sb("slot", [P, 4, 2, 2], I32)
        prow = s.sb("prow", [P, 4, 2], I32)
        x = s.sb("x", [P, 2, 2, D])
        xT = s.sb("xT", [P, 2, DC, CAP])
        act_g = s.sb("act_g", [P, 2, FC, CAP])
        h = s.sb("h", [P, FC, CAP])
        h_hi, h_lo = s.sb("h_hi", [P, 2, FC, 2 * P], F32R), s.sb("h_lo", [P, 2, FC, 2 * P], F32R)
        y = s.sb("y", [P, 2, 2, D])
        T = s.ps("T", [P, 2, 512])
        G = s.ps("G", [P, 2, 512])
        U = s.ps("U", [P, 2, 512])
        Y = s.ps("Y", [P, 2, 512])

        consts = s.sem("consts")
        held = s.sem("held")
        slot_in = s.sems("slot_in", 4)
        listed = s.sem("listed")
        gu_in = s.sems("gu_in", 2)
        d_in = s.sems("d_in", 2)
        x_in = s.sems("x_in", 2)
        flipped = s.sem("flipped")
        x_act = s.sem("x_act")
        x_dve = s.sem("x_dve")
        gated = s.sem("gated")
        silued = s.sem("silued")
        h_ready = s.sem("h_ready")
        d_high, d_split = s.sem("d_high"), s.sem("d_split")
        downed = s.sem("downed")
        y_act = s.sem("y_act")
        y_dve = s.sem("y_dve")
        y_out = s.sems("y_out", 2)

        slots = dram["slot"][0:EXPERTS * STRIDE, :].rearrange("(e r) a -> e r a", r=STRIDE)

        def pick(t, e):
            return t[e.c] if e.turn is None else t[bass.ds(e.n, 1)].rearrange("a p n -> (a p) n")

        with nc.Block() as block:
            @block.sync
            def _(sp):
                sp.dma_start(ident[:, :], io["ident"]).then_inc(consts, 16)

                def slots_of(e):
                    if e.after(4):
                        sp.wait_ge(listed, e.back(4).count(1, 1))
                    for t, (lo, n) in enumerate(TC):
                        sp.dma_start(slot[0:n, e.slot4, t, :], pick(slots[:, lo:lo + n, :], e)).then_inc(slot_in[e.slot4], 16)

                def step(e):
                    if e.c == 0:
                        slots_of(e)
                        slots_of(e.back(-1))
                    if e.back(-2).live(EXPERTS):
                        slots_of(e.back(-2))
                    if e.live(EXPERTS):
                        if e.after(2):
                            sp.wait_ge(gated, e.back(2).count(1, 1))
                        sp.dma_start(wg[:, e.slot, :, :].rearrange("p c f -> p (c f)"),
                                     pick(io["moe_w_gate"][layer].rearrange("e (p c) f -> e p (c f)", c=DC), e)).then_inc(gu_in[e.slot], 16)
                        sp.dma_start(wu[:, e.slot, :, :].rearrange("p c f -> p (c f)"),
                                     pick(io["moe_w_up"][layer].rearrange("e (p c) f -> e p (c f)", c=DC), e)).then_inc(gu_in[e.slot], 16)
                    f = e.back(1)
                    if f.live(EXPERTS):
                        if f.after(2):
                            sp.wait_ge(d_split, f.back(2).count(1, 1))
                        sp.dma_start(wd[:, f.slot, :],
                                     pick(io["moe_w_down"][layer].rearrange("e (p c) f -> e p (c f)", c=FC), f)).then_inc(d_in[f.slot], 16)
                over_steps(sp, 0, 1 + EXPERTS, 6, EXPERTS - 2, step, unroll=4)

            @block.gpsimd
            def _(pool):
                nc.gpsimd.memset(prow[:, :, :], 2 * ROWS)
                pool.drain()

                def gather(e):
                    pool.wait_ge(slot_in[e.slot4], (e.uses4 + 1) * 32)
                    if e.after(2):
                        pool.wait_ge(flipped, e.back(2).count(3, 3))
                    if e.after(4):
                        pool.wait_ge(y_out[e.slot], e.back(2).uses * 32)
                    pool.sem_inc(held, 1)
                    for t, (lo, n) in enumerate(TC):
                        pool.indirect_dma_start(x[0:n, e.slot, t, :], None, dram["xn"],
                                                bass.IndirectOffsetOnAxis(ap=slot[0:n, e.slot4, t, 0:1], axis=0)).then_inc(x_in[e.slot], 16)
                    for t, (lo, n) in enumerate(TC):
                        nc.gpsimd.tensor_copy(prow[0:n, e.slot4, t:t + 1], slot[0:n, e.slot4, t, 1:2])
                    pool.wait_ge(x_in[e.slot], (e.uses + 1) * 32)
                    pool.sem_inc(held, 1)
                    pool.drain().then_inc(listed, 1)

                def step(e):
                    if e.c == 0:
                        gather(e)
                    if e.back(-1).live(EXPERTS):
                        gather(e.back(-1))
                    f = e.back(2)
                    if f.live(EXPERTS):
                        pool.wait_ge(y_act, f.count(2, 2))
                        pool.wait_ge(y_dve, f.count(2, 2))
                        pool.sem_inc(held, 1)
                        for t, (lo, n) in enumerate(TC):
                            pool.indirect_dma_start(dram["y"], bass.IndirectOffsetOnAxis(ap=prow[0:n, f.slot4, t:t + 1], axis=0),
                                                    y[0:n, f.slot, t, :], None, bounds_check=2 * ROWS - 1, oob_is_err=False).then_inc(y_out[f.slot], 16)
                over_steps(pool, 0, 2 + EXPERTS, 6, EXPERTS - 2, step, unroll=4)
                for b in range(2):
                    pool.wait_ge(y_out[b], 32 * (EXPERTS // 2))

            @block.scalar
            def _(act):
                def step(e):
                    if e.live(EXPERTS):
                        for b in (0, 2):
                            lo, hi = XB[b]
                            act.wait_ge(flipped, e.count(3, b + 1))
                            nc.scalar.copy(xT[:, e.slot, lo:hi, :].rearrange("p c t -> p (c t)"), T[:, (b % 2 + e.c) % 2, 0:CAP * (hi - lo)]).then_inc(x_act, 1)
                    f, g = e.back(1), e.back(2)
                    if g.live(EXPERTS):
                        act.wait_ge(d_in[g.slot], (g.uses + 1) * 16)
                        if g.after(1):
                            act.wait_ge(downed, g.back(1).count(4, 4))
                        nc.scalar.copy(wd_hi[:, :, :].rearrange("p c f -> p (c f)"), wd[:, g.slot, :]).then_inc(d_high, 1)
                    if f.live(EXPERTS):
                        act.wait_ge(gated, f.count(1, 1))
                        if f.after(2):
                            act.wait_ge(h_ready, f.back(2).count(1, 1))
                        nc.scalar.activation(act_g[:, f.slot, :, :].rearrange("p c t -> p (c t)"), G[:, f.slot, 0:FC * CAP], ACT.Silu).then_inc(silued, 1)
                    if g.live(EXPERTS):
                        if g.after(2):
                            act.wait_ge(y_out[g.slot], g.uses * 32)
                        for t, (lo, n) in enumerate(TC):
                            act.wait_ge(downed, g.count(4, 2 * t + 1))
                            nc.scalar.copy(y[0:n, g.slot, t, 0:512], Y[0:n, 0, :]).then_inc(y_act, 1)
                over_steps(act, 0, 2 + EXPERTS, 4, EXPERTS, step, unroll=4)

            @block.vector
            def _(dve):
                nc.vector.memset(h_hi[:, :, :, :].rearrange("p a c t -> p (a c t)").bitcast(F32), 0.0)
                nc.vector.memset(h_lo[:, :, :, :].rearrange("p a c t -> p (a c t)").bitcast(F32), 0.0)
                dve.drain()

                def low_part(low, whole, high):
                    return nc.vector.tensor_tensor(low, whole, high.bitcast(F32), ALU.subtract)

                def step(e):
                    if e.live(EXPERTS):
                        lo, hi = XB[1]
                        dve.wait_ge(flipped, e.count(3, 2))
                        nc.vector.tensor_copy(xT[:, e.slot, lo:hi, :].rearrange("p c t -> p (c t)"), T[:, (1 + e.c) % 2, 0:CAP * (hi - lo)]).then_inc(x_dve, 1)
                    f, g = e.back(1), e.back(2)
                    if g.live(EXPERTS):
                        dve.wait_ge(d_high, g.count(1, 1))
                        low_part(wd_lo[:, :, :].rearrange("p c f -> p (c f)"), wd[:, g.slot, :], wd_hi[:, :, :].rearrange("p c f -> p (c f)")).then_inc(d_split, 1)
                    if f.live(EXPERTS):
                        if f.after(1):
                            dve.wait_ge(h_ready, f.count(1, 0))
                        dve.wait_ge(silued, f.count(1, 1))
                        nc.vector.tensor_tensor(h[:, :, :].rearrange("p c t -> p (c t)"), act_g[:, f.slot, :, :].rearrange("p c t -> p (c t)"),
                                                U[:, f.slot, 0:FC * CAP], ALU.mult)
                        dve.drain()
                        if f.after(2):
                            dve.wait_ge(downed, f.back(2).count(4, 4))
                        nc.vector.tensor_copy(h_hi[:, f.slot, :, 0:CAP], h[:, :, :])
                        dve.drain()
                        low_part(h_lo[:, f.slot, :, 0:CAP], h[:, :, :], h_hi[:, f.slot, :, 0:CAP]).then_inc(h_ready, 1)
                    if g.live(EXPERTS):
                        if g.after(2):
                            dve.wait_ge(y_out[g.slot], g.uses * 32)
                        for t, (lo, n) in enumerate(TC):
                            dve.wait_ge(downed, g.count(4, 2 * t + 2))
                            nc.vector.tensor_copy(y[0:n, g.slot, t, 512:D], Y[0:n, 1, :]).then_inc(y_dve, 1)
                over_steps(dve, 0, 2 + EXPERTS, 4, EXPERTS, step, unroll=4)

            @block.tensor
            def _(pe):
                pe.wait_ge(consts, 16)

                def step(e):
                    if e.live(EXPERTS):
                        pe.wait_ge(x_in[e.slot], (e.uses + 1) * 32)
                        for b, (lo, hi) in enumerate(XB):
                            if b == 0 and e.after(1):
                                pe.wait_ge(x_dve, e.count(1, 0))
                            if b == 1 and e.after(1):
                                pe.wait_ge(x_act, e.count(2, 0))
                            if b == 2:
                                pe.wait_ge(x_act, e.count(2, 1))
                            for c in range(lo, hi):
                                for t, (at, n) in enumerate(TC):
                                    xc = x[0:n, e.slot, t, :].rearrange("p (q c) -> p c q", c=DC)[:, c, :]
                                    last = nc.tensor.transpose(T[:, (b + e.c) % 2, CAP * (c - lo) + at:CAP * (c - lo) + at + n], xc, ident[0:n, 0:n])
                            last.then_inc(flipped, 1)
                    f = e.back(1)
                    if f.live(EXPERTS):
                        pe.wait_ge(gu_in[f.slot], (f.uses + 1) * 32)
                        pe.wait_ge(x_act, f.count(2, 2))
                        pe.wait_ge(x_dve, f.count(1, 1))
                        if f.after(2):
                            pe.wait_ge(h_ready, f.back(2).count(1, 1))
                        for w, out in ((wg, G), (wu, U)):
                            for k in range(FC):
                                for c in range(DC):
                                    wk = w[:, f.slot, c, :].rearrange("p (q k) -> p k q", k=FC)[:, k, :]
                                    last = nc.tensor.matmul(out[:, f.slot, CAP * k:CAP * k + CAP], wk, xT[:, f.slot, c, :],
                                                            start=(c == 0), stop=(c == DC - 1))
                        last.then_inc(gated, 1)
                    g = e.back(2)
                    if g.live(EXPERTS):
                        pe.wait_ge(d_split, g.count(1, 1))
                        pe.wait_ge(h_ready, g.count(1, 1))
                        for t in range(len(TC)):
                            for b in range(2):
                                if t == 1 or g.after(1):
                                    pe.wait_ge(y_dve if b else y_act, g.count(2, t))
                                for k in range(FC):
                                    hi, lo = h_hi[:, g.slot, k, P * t:P * t + P], h_lo[:, g.slot, k, P * t:P * t + P]
                                    w = slice(512 * b, 512 * b + 512)
                                    nc.tensor.matmul(Y[:, b, :], hi, wd_hi[:, k, w], start=(k == 0), stop=False)
                                    nc.tensor.matmul(Y[:, b, :], hi, wd_lo[:, k, w], start=False, stop=False)
                                    last = nc.tensor.matmul(Y[:, b, :], lo, wd_hi[:, k, w], start=False, stop=(k == FC - 1))
                                last.then_inc(downed, 1)
                over_steps(pe, 0, 2 + EXPERTS, 4, EXPERTS, step, unroll=4)


def combine_and_project_b(nc, io, dram, keep):
    with ExitStack() as ctx:
        s = Space(nc, ctx, "pb")
        win = s.sb("win", [P, DC, B_IN])
        wuq = s.sb("wuq", [P, QR // P, HEADS * QD])
        wuk = s.sb("wuk", [P, HEADS * HD])
        wuv = s.sb("wuv", [P, HEADS * HD])
        gain = s.sb("gain", [P, D])
        gq = s.sb("gq", [P, QR])
        gkv = s.sb("gkv", [P, KVR])
        ident = s.sb("ident", [P, P])
        half = s.sb("half", [P, 2])
        h = s.sb("h", [P, 2, D])
        y = s.sb("y", [P, 2, 2, D])
        cs = s.sb("cs", [P, 4, 2 * ROPE])
        hsq = s.sb("hsq", [P, D])
        ssq = s.sb("ssq", [P, 2])
        rstd = s.sb("rstd", [P, 2])
        xn = s.sb("xn", [P, D])
        xT = s.sb("xT", [P, DC, P])
        c = s.sb("c", [P, 2, B_IN])
        cssq = s.sb("cssq", [P, 2, 2])
        crstd = s.sb("crstd", [P, 2, 2])
        cn = s.sb("cn", [P, 2, QR + KVR])
        kpe = s.sb("kpe", [P, 2, ROPE])
        krot = s.sb("krot", [P, ROPE])
        cT = s.sb("cT", [P, 3, P])
        kpeT = s.sb("kpeT", [ROPE, 2, P])
        q = s.sb("q", [P, 2, HEADS * QD])
        qrot = s.sb("qrot", [P, HEADS, ROPE])
        qT = s.sb("qT", [QD, 2, HEADS, P])
        kT = s.sb("kT", [P, 2, DC, P])
        v = s.sb("v", [P, 2, HEADS * HD])
        B = s.ps("B", [P, 8, 512])

        consts = s.sem("consts")
        held = s.sem("held")
        passed = s.sem("passed")
        h_in, y_in, cs_in = s.sems("h_in", 2), s.sems("y_in", 2), s.sems("cs_in", 4)
        summed = s.sem("summed")
        squared = s.sem("squared")
        rstd_ready = s.sem("rstd_ready")
        xn_ready = s.sem("xn_ready")
        flipped = s.sem("flipped")
        x_act, x_dve = s.sem("x_act"), s.sem("x_dve")
        latent = s.sem("latent")
        c_ready = s.sem("c_ready")
        csquared = s.sem("csquared")
        crstd_ready = s.sem("crstd_ready")
        cn_ready = s.sem("cn_ready")
        kpe_ready = s.sem("kpe_ready")
        cflipped = s.sem("cflipped")
        cT_ready = s.sem("cT_ready")
        kp = s.sem("kp")
        vp = s.sem("vp")
        qp = s.sem("qp")
        k_act, k_dve, v_act, v_dve, q_act, q_dve = (s.sem(n) for n in ("k_act", "k_dve", "v_act", "v_dve", "q_act", "q_dve"))
        roped = s.sem("roped")
        qflipped = s.sem("qflipped")
        qT_act, qT_dve = s.sem("qT_act"), s.sem("qT_dve")
        h_out, k_out, v_out, q_out = (s.sems(n, 2) for n in ("h_out", "k_out", "v_out", "q_out"))
        NCONST = 8

        def columns(i):
            if i.turn is None:
                return slice(0, META) if i.c == 0 else slice(META + (i.c - 1) * P, META + i.c * P)
            return bass.ds(i.n * P - (P - META), P)

        with nc.Block() as block:
            @block.sync
            def _(sp):
                sp.dma_start(gain[:, :], bcast(io["attn_norm"][1, :], D)).then_inc(consts, 16)
                sp.dma_start(gq[:, :], bcast(io["b_q_norm"][0, :], QR)).then_inc(consts, 16)
                sp.dma_start(gkv[:, :], bcast(io["b_kv_norm"][0, :], KVR)).then_inc(consts, 16)
                sp.dma_start(ident[:, :], io["ident"]).then_inc(consts, 16)
                sp.dma_start(win[:, :, :], io["b_w_in"][0].rearrange("(c p) n -> p c n", p=P)).then_inc(consts, 16)
                sp.dma_start(wuq[:, :, :], io["b_w_uq"][0].rearrange("(c p) n -> p c n", p=P)).then_inc(consts, 16)
                ukv = io["b_w_ukv"][0].rearrange("p (h a d) -> p h a d", a=2, d=HD)
                sp.dma_start(wuk[:, :].rearrange("p (h d) -> p h d", d=HD), ukv[:, :, 0, :]).then_inc(consts, 16)
                sp.dma_start(wuv[:, :].rearrange("p (h d) -> p h d", d=HD), ukv[:, :, 1, :]).then_inc(consts, 16)

                def load(i):
                    if i.after(2):
                        sp.wait_ge(xn_ready, i.back(2).count(1, 1))
                        sp.wait_ge(h_out[i.slot], i.uses * 16)
                    sp.dma_start(h[:, i.slot, :], rows(dram["h"], i)).then_inc(h_in[i.slot], 16)
                    sp.dma_start(y[:, i.slot, :, :].rearrange("p k d -> p (k d)"),
                                 rows(dram["y"].rearrange("(r k) d -> r (k d)", k=2), i)).then_inc(y_in[i.slot], 16)
                    if i.after(4):
                        sp.wait_ge(roped, i.back(4).count(1, 1))
                    sp.dma_start(cs[:, i.slot4, :], rows(io["cs_b"], i)).then_inc(cs_in[i.slot4], 16)

                def step(i):
                    if i.turn is None and i.c == 0:
                        load(i)
                        load(i.back(-1))
                    if i.live():
                        sp.wait_ge(summed, i.count(1, 1))
                        sp.dma_start(rows(dram["h"], i), h[:, i.slot, :]).then_inc(h_out[i.slot], 16)
                    j = i.back(2)
                    if j.live():
                        sp.wait_ge(k_act, j.count(1, 1))
                        sp.wait_ge(k_dve, j.count(1, 1))
                        n = META if (j.turn is None and j.c == 0) else P
                        for a in range(2):
                            sp.dma_start(dram["kT"].rearrange("(c a) d t -> a d c t", a=2)[a][:, :, columns(j)],
                                         kT[HD * a:HD * a + HD, j.slot, :, 0:n]).then_inc(k_out[j.slot], 16)
                        sp.wait_ge(cT_ready, j.count(1, 1))
                        sp.dma_start(dram["kpeT"][:, columns(j)], kpeT[:, j.slot, 0:n]).then_inc(k_out[j.slot], 16)
                        sp.wait_ge(v_act, j.count(1, 1))
                        sp.wait_ge(v_dve, j.count(1, 1))
                        sp.dma_start(dram["v"].rearrange("h p t d -> t p h d")[tile_at(j)].rearrange("a p h d -> (a p) h d"),
                                     v[:, j.slot, :].rearrange("p (h d) -> p h d", d=HD)).then_inc(v_out[j.slot], 16)
                    k = i.back(3)
                    if k.live():
                        sp.wait_ge(qT_act, k.count(2, 2))
                        sp.wait_ge(qT_dve, k.count(2, 2))
                        sp.sem_inc(passed, 1)
                        sp.dma_start(dram["qT"].rearrange("h d (t q) -> t d h q", q=P)[tile_at(k)].rearrange("a d h q -> (a d) h q"),
                                     qT[:, k.slot, :, :]).then_inc(q_out[k.slot], 16)
                    if i.back(-2).live() and i.after(0):
                        load(i.back(-2))
                over_steps(sp, 0, 3 + NT, 4, NT - 5, step, unroll=4)
                for b in range(2):
                    n = (NT + 1 - b) // 2
                    sp.wait_ge(h_out[b], 16 * n)
                    sp.wait_ge(k_out[b], 48 * n)
                    sp.wait_ge(v_out[b], 16 * n)
                    sp.wait_ge(q_out[b], 16 * n)

            @block.gpsimd
            def _(pool):
                nc.gpsimd.memset(half[:, :], -0.5)
                pool.drain()

                def rope(x, rot, out, i, n):
                    t = cs[:, i.slot4, :]
                    e = ROPE // 2
                    cos, nsin, sin = (t[:, a:b].unsqueeze(1).to_broadcast([P, n, b - a]) for a, b in
                                      ((0, ROPE), (ROPE, ROPE + e), (ROPE + e, 2 * ROPE)))
                    nc.gpsimd.tensor_tensor(rot[:, :, 0:e], x[:, :, e:ROPE], nsin, ALU.mult)
                    nc.gpsimd.tensor_tensor(rot[:, :, e:ROPE], x[:, :, 0:e], sin, ALU.mult)
                    pool.drain()
                    nc.gpsimd.tensor_tensor(out, x, cos, ALU.mult)
                    pool.drain()
                    nc.gpsimd.tensor_tensor(out, out, rot, ALU.add)

                def step(i):
                    k = i.back(2)
                    if k.live():
                        pool.wait_ge(q_act, k.count(2, 2))
                        pool.wait_ge(q_dve, k.count(1, 1))
                        x = q[:, k.slot, :].rearrange("p (h d) -> p h d", d=QD)[:, :, HD:QD]
                        rope(x, qrot[:, :, :], x, k, HEADS)
                        pool.drain().then_inc(roped, 1)
                    h_next = i.back(-1)
                    if h_next.live():
                        pool.wait_ge(squared, h_next.count(1, 1))
                        pool.sem_inc(held, 1)
                        r = rstd[:, h_next.slot:h_next.slot + 1]
                        nc.gpsimd.tensor_scalar(r, ssq[:, h_next.slot:h_next.slot + 1], 1.0 / D, EPS, ALU.mult, ALU.add)
                        pool.drain()
                        nc.gpsimd.tensor_tensor(r, r, half[:, 0:1], ALU.pow).then_inc(rstd_ready, 1)
                    if i.live():
                        pool.wait_ge(csquared, i.count(1, 1))
                        pool.sem_inc(held, 1)
                        for a, n in ((0, QR), (1, KVR)):
                            nc.gpsimd.tensor_scalar(crstd[:, i.slot, a:a + 1], cssq[:, i.slot, a:a + 1], 1.0 / n, EPS, ALU.mult, ALU.add)
                        pool.drain()
                        nc.gpsimd.tensor_tensor(crstd[:, i.slot, :], crstd[:, i.slot, :], half[:, :], ALU.pow).then_inc(crstd_ready, 1)
                        pool.wait_ge(cs_in[i.slot4], (i.uses4 + 1) * 16)
                        if i.after(2):
                            pool.wait_ge(cflipped, i.back(2).count(1, 1))
                        rope(c[:, i.slot, QR + KVR:B_IN].rearrange("p (a d) -> p a d", a=1), krot[:, :].rearrange("p (a d) -> p a d", a=1),
                             kpe[:, i.slot, :].rearrange("p (a d) -> p a d", a=1), i, 1)
                        pool.drain().then_inc(kpe_ready, 1)
                over_steps(pool, -1, 2 + NT, 4, NT - 1, step, unroll=4)

            @block.scalar
            def _(act):
                act.wait_ge(consts, 16 * NCONST)

                def step(i):
                    if i.live():
                        act.wait_ge(flipped, i.count(2, 1))
                        nc.scalar.copy(xT[:, 0:4, :].rearrange("p c t -> p (c t)"), B[:, 0, :]).then_inc(x_act, 1)
                    h_next = i.back(-1)
                    if h_next.live():
                        act.wait_ge(summed, h_next.count(1, 1))
                        nc.scalar.activation(hsq[:, :], h[:, h_next.slot, :], ACT.Square, accum_out=ssq[:, h_next.slot:h_next.slot + 1])
                        act.drain().then_inc(squared, 1)
                    if i.live():
                        act.wait_ge(latent, i.count(1, 1))
                        if i.after(2):
                            act.wait_ge(cn_ready, i.back(2).count(1, 1))
                            act.wait_ge(kpe_ready, i.back(2).count(1, 1))
                        nc.scalar.copy(c[:, i.slot, :], B[:, 2, 0:B_IN]).then_inc(c_ready, 1)
                        act.drain()
                        nc.scalar.activation(hsq[:, 0:QR], c[:, i.slot, 0:QR], ACT.Square, accum_out=cssq[:, i.slot, 0:1])
                        nc.scalar.activation(hsq[:, QR:QR + KVR], c[:, i.slot, QR:QR + KVR], ACT.Square, accum_out=cssq[:, i.slot, 1:2])
                        act.drain().then_inc(csquared, 1)
                    j = i.back(1)
                    if j.live():
                        act.wait_ge(kp, j.count(2, 1))
                        if j.after(2):
                            act.wait_ge(k_out[j.slot], j.uses * 48)
                        nc.scalar.copy(kT[:, j.slot, 0:4, :].rearrange("p c t -> p (c t)"), B[:, 4, :]).then_inc(k_act, 1)
                        act.wait_ge(vp, j.count(2, 1))
                        if j.after(2):
                            act.wait_ge(v_out[j.slot], j.uses * 16)
                        nc.scalar.copy(v[:, j.slot, 0:512], B[:, 6, :]).then_inc(v_act, 1)
                        for a in (0, 2):
                            act.wait_ge(qp, j.count(3, a + 1))
                            nc.scalar.copy(q[:, j.slot, 512 * a:512 * a + 512], B[:, a, :]).then_inc(q_act, 1)
                    k = i.back(2)
                    if k.live():
                        for a in (0, 2):
                            act.wait_ge(qflipped, k.count(4, a + 1))
                            if a == 0 and k.after(2):
                                act.wait_ge(q_out[k.slot], k.uses * 16)
                            nc.scalar.copy(qT[:, k.slot, 4 * a:4 * a + 4, :].rearrange("p c t -> p (c t)"), B[0:QD, 3 + a, :]).then_inc(qT_act, 1)
                over_steps(act, -1, 2 + NT, 4, NT - 1, step, unroll=4)

            @block.vector
            def _(dve):
                dve.wait_ge(consts, 16 * NCONST)

                def normalise(i):
                    dve.wait_ge(h_in[i.slot], (i.uses + 1) * 16)
                    dve.wait_ge(y_in[i.slot], (i.uses + 1) * 16)
                    for k in range(2):
                        w = keep["weights"][:, :, k][:, tile_at(i)]
                        nc.vector.scalar_tensor_tensor(out=h[:, i.slot, :], in0=y[:, i.slot, k, :], scalar=w, in1=h[:, i.slot, :],
                                                       op0=ALU.mult, op1=ALU.add)
                        if k == 0:
                            dve.drain()
                    dve.drain().then_inc(summed, 1)
                    dve.wait_ge(rstd_ready, i.count(1, 1))
                    if i.after(1):
                        dve.wait_ge(flipped, i.back(1).count(2, 2))
                    nc.vector.scalar_tensor_tensor(out=xn[:, :], in0=h[:, i.slot, :], scalar=rstd[:, i.slot:i.slot + 1],
                                                   in1=gain[:, :], op0=ALU.mult, op1=ALU.mult).then_inc(xn_ready, 1)

                def step(i):
                    if i.live():
                        dve.wait_ge(flipped, i.count(2, 2))
                        nc.vector.tensor_copy(xT[:, 4:8, :].rearrange("p c t -> p (c t)"), B[:, 1, :]).then_inc(x_dve, 1)
                    if i.back(-1).live():
                        normalise(i.back(-1))
                    j = i.back(1)
                    if j.live():
                        dve.wait_ge(cflipped, j.count(1, 1))
                        nc.vector.tensor_copy(cT[:, :, :].rearrange("p c t -> p (c t)"), B[:, 3, 0:3 * P])
                        if j.after(2):
                            dve.wait_ge(k_out[j.slot], j.uses * 48)
                        nc.vector.tensor_copy(kpeT[:, j.slot, :], B[0:ROPE, 3, 3 * P:4 * P])
                        dve.drain().then_inc(cT_ready, 1)
                        dve.wait_ge(kp, j.count(2, 2))
                        nc.vector.tensor_copy(kT[:, j.slot, 4:8, :].rearrange("p c t -> p (c t)"), B[:, 5, :]).then_inc(k_dve, 1)
                        dve.wait_ge(vp, j.count(2, 2))
                        if j.after(2):
                            dve.wait_ge(v_out[j.slot], j.uses * 16)
                        nc.vector.tensor_copy(v[:, j.slot, 512:D], B[:, 7, :]).then_inc(v_dve, 1)
                        dve.wait_ge(qp, j.count(3, 2))
                        nc.vector.tensor_copy(q[:, j.slot, 512:D], B[:, 1, :]).then_inc(q_dve, 1)
                    if i.live():
                        dve.wait_ge(crstd_ready, i.count(1, 1))
                        if i.after(2):
                            dve.wait_ge(cflipped, i.back(2).count(1, 1))
                        nc.vector.scalar_tensor_tensor(out=cn[:, i.slot, 0:QR], in0=c[:, i.slot, 0:QR], scalar=crstd[:, i.slot, 0:1],
                                                       in1=gq[:, :], op0=ALU.mult, op1=ALU.mult)
                        nc.vector.scalar_tensor_tensor(out=cn[:, i.slot, QR:QR + KVR], in0=c[:, i.slot, QR:QR + KVR], scalar=crstd[:, i.slot, 1:2],
                                                       in1=gkv[:, :], op0=ALU.mult, op1=ALU.mult)
                        dve.drain().then_inc(cn_ready, 1)
                    k = i.back(2)
                    if k.live():
                        for a in (1, 3):
                            dve.wait_ge(qflipped, k.count(4, a + 1))
                            if a == 1 and k.after(2):
                                dve.wait_ge(q_out[k.slot], k.uses * 16)
                            nc.vector.tensor_copy(qT[:, k.slot, 4 * a:4 * a + 4, :].rearrange("p c t -> p (c t)"), B[0:QD, 3 + a, :]).then_inc(qT_dve, 1)
                over_steps(dve, -1, 2 + NT, 4, NT - 1, step, unroll=4)

            @block.tensor
            def _(pe):
                pe.wait_ge(consts, 16 * NCONST)

                def step(i):
                    if i.live():
                        pe.wait_ge(xn_ready, i.count(1, 1))
                        for b in range(2):
                            if i.after(2):
                                pe.wait_ge(q_dve if b else q_act, i.back(2).count(1 if b else 2, 1))
                            for cc in range(4 * b, 4 * b + 4):
                                last = nc.tensor.transpose(B[:, b, P * (cc % 4):P * (cc % 4) + P], xn[:, P * cc:P * cc + P], ident[:, :])
                            last.then_inc(flipped, 1)
                        pe.wait_ge(x_act, i.count(1, 1))
                        pe.wait_ge(x_dve, i.count(1, 1))
                        if i.after(2):
                            pe.wait_ge(q_act, i.back(2).count(2, 2))
                        for cc in range(DC):
                            last = nc.tensor.matmul(B[:, 2, 0:B_IN], xT[:, cc, :], win[:, cc, :], start=(cc == 0), stop=(cc == DC - 1))
                        last.then_inc(latent, 1)
                    j = i.back(1)
                    if j.live():
                        pe.wait_ge(cn_ready, j.count(1, 1))
                        pe.wait_ge(kpe_ready, j.count(1, 1))
                        if j.after(2):
                            pe.wait_ge(qT_act, j.back(2).count(2, 1))
                        for cc in range(3):
                            nc.tensor.transpose(B[:, 3, P * cc:P * cc + P], cn[:, j.slot, P * cc:P * cc + P], ident[:, :])
                        nc.tensor.transpose(B[0:ROPE, 3, 3 * P:4 * P], kpe[:, j.slot, :], ident[:, :]).then_inc(cflipped, 1)
                        pe.wait_ge(cT_ready, j.count(1, 1))
                        for b in range(2):
                            if j.after(2):
                                pe.wait_ge(qT_act if b else qT_dve, j.back(2).count(2, 2 if b else 1))
                            for cc in range(4):
                                at = P * (4 * b + cc)
                                last = nc.tensor.matmul(B[:, 4 + b, P * cc:P * cc + P], wuk[:, at:at + P], cT[:, 2, :], start=True, stop=True)
                            last.then_inc(kp, 1)
                        for b in range(2):
                            if j.after(2):
                                if b == 0:
                                    pe.wait_ge(qT_dve, j.back(2).count(2, 2))
                                else:
                                    pe.wait_ge(v_dve, j.back(1).count(1, 1))
                            elif j.after(1) and b == 1:
                                pe.wait_ge(v_dve, 1)
                            last = nc.tensor.matmul(B[:, 6 + b, :], cT[:, 2, :], wuv[:, 512 * b:512 * b + 512], start=True, stop=True)
                            last.then_inc(vp, 1)
                        for b in range(3):
                            if b == 0:
                                pe.wait_ge(x_act, i.count(1, 1) if i.live() else NT)
                            if b == 1:
                                pe.wait_ge(x_dve, i.count(1, 1) if i.live() else NT)
                            if b == 2:
                                pe.wait_ge(c_ready, i.count(1, 1) if i.live() else NT)
                            for cc in range(2):
                                last = nc.tensor.matmul(B[:, b, :], cT[:, cc, :], wuq[:, cc, 512 * b:512 * b + 512], start=(cc == 0), stop=(cc == 1))
                            last.then_inc(qp, 1)
                    k = i.back(2)
                    if k.live():
                        pe.wait_ge(roped, k.count(1, 1))
                        for a in range(4):
                            if j.live():
                                pe.wait_ge((cT_ready, k_act, k_dve, v_act)[a], j.count(1, 1))
                            else:
                                pe.wait_ge((qT_act, qT_dve)[a % 2], k.count(2, -1 + a // 2))
                            for hh in range(4):
                                n = 4 * a + hh
                                last = nc.tensor.transpose(B[0:QD, 3 + a, P * hh:P * hh + P], q[:, k.slot, QD * n:QD * n + QD], ident[:, :])
                            last.then_inc(qflipped, 1)
                over_steps(pe, 0, 2 + NT, 4, NT - 1, step, unroll=4)


def attention_b(nc, io, dram):
    PAIRS = HEADS // 2
    CK = 4
    NC = 1 + NT // CK
    units = []
    for t in range(NT):
        pieces = [(0, META, 0)] + [(META + P * (b - 1), P, b) for b in range(1, t + 1)]
        for c in range(NC):
            mine = [p for p in pieces if p[2] // CK == c]
            if mine:
                lo = mine[0][0]
                units.append((t, c, lo, sum(p[1] for p in mine), [(p[0] - lo, p[1], p[2]) for p in mine]))
    NU = len(units)
    pair_units = [(hs, *u) for hs in range(2) for u in units]
    PU = 2 * NU
    chunks_of = [sum(u[0] == t for u in units) for t in range(NT)]

    with ExitStack() as ctx:
        s = Space(nc, ctx, "ab")
        ident = s.sb("ident", [P, P])
        identb = s.sb("identb", [P, P], BF16)
        mask = s.sb("mask", [P, P], BF16)
        qT = s.sb("qT", [QD, 2, ROWS])
        kT = s.sb("kT", [QD, 2, KEYS])
        v = s.sb("v", [P, 2, NT, HD])
        prob = s.sb("prob", [P, 3, 512])
        pT = s.sb("pT", [P, 3, 512])
        mx = s.sb("mx", [P, 3])
        neg = s.sb("neg", [P, 2, NC, NT])
        total = s.sb("total", [P, 2, NC, NT])
        part = s.sb("part", [P, 2, NC, NT, HD])
        low = s.sb("low", [P, NT])
        w = s.sb("w", [P, 2, NC, NT])
        wt = s.sb("wt", [P, NC, NT])
        den = s.sb("den", [P, NT])
        tmp = s.sb("tmp", [P, NT, HD])
        acc = s.sb("acc", [P, NT, HD])
        o = s.sb("o", [P, NT, 2, HD])
        S = s.ps("S", [P, 3, 512])
        PT = s.ps("PT", [P, 3, 512])
        O = s.ps("O", [P, 2, 512])

        consts = s.sem("consts")
        NCONST = 5
        cleared = s.sem("cleared")
        qk_in = s.sems("qk_in", 2)
        v_in = s.sems("v_in", 2)
        scored = s.sem("scored")
        maxed = s.sem("maxed")
        exped = s.sem("exped")
        flipped = s.sem("flipped")
        pT_dve = s.sem("pT_dve")
        pT_act = s.sem("pT_act")
        summed = s.sem("summed")
        parted = s.sem("parted")
        w_in = s.sem("w_in")
        w_exped = s.sem("w_exped")
        w_ready = s.sem("w_ready")
        combined = s.sem("combined")
        o_out = s.sem("o_out")

        def head(t, pair, hs):
            if pair.turn is None:
                return t[2 * pair.c + hs]
            return t[bass.ds(pair.n * 2 + hs, 1)].rearrange("a p n -> (a p) n")

        def pairs(eng, body):
            over_steps(eng, 0, PAIRS, 1, PAIRS, body, unroll=1)

        def copier(u):
            return (pT_act if u % 2 else pT_dve), u // 2 + 1

        with nc.Block() as block:
            @block.sync
            def _(sp):
                sp.dma_start(ident[:, :], io["ident"]).then_inc(consts, 16)
                sp.dma_start(identb[:, :], io["identb"]).then_inc(consts, 16)
                sp.dma_start(mask[:, :], io["mask_b"]).then_inc(consts, 16)
                for hs in range(2):
                    sp.dma_start(kT[HD:QD, hs, :], dram["kpeT"]).then_inc(consts, 16)

                def body(pair):
                    for hs in range(2):
                        if pair.after(1):
                            sp.wait_ge(scored, pair.count(PU, NU * (hs + 1) - PU))
                        sp.dma_start(qT[:, hs, :], head(dram["qT"], pair, hs)).then_inc(qk_in[hs], 16)
                        sp.dma_start(kT[0:HD, hs, :], head(dram["kT"], pair, hs)).then_inc(qk_in[hs], 16)
                        if pair.after(1):
                            sp.wait_ge(summed, pair.count(PU, NU * (hs + 1) - PU))
                        sp.dma_start(v[:, hs, :, :].rearrange("p t d -> p (t d)"),
                                     head(dram["v"].rearrange("h p t d -> h p (t d)"), pair, hs)).then_inc(v_in[hs], 16)
                    b = pair.back(1)
                    if b.after(0):
                        store(b)

                def store(b):
                    sp.wait_ge(combined, b.count(2, 2))
                    cols = slice(b.c * P, b.c * P + P) if b.turn is None else bass.ds(b.n * P, P)
                    sp.dma_start(dram["o"].rearrange("(t p) d -> p t d", p=P)[:, :, cols],
                                 o[:, :, :, :].rearrange("p t a d -> p t (a d)")).then_inc(o_out, 16)
                pairs(sp, body)
                store(At(None, PAIRS - 1))
                sp.wait_ge(o_out, 16 * PAIRS)

            @block.gpsimd
            def _(pool):
                nc.gpsimd.memset(neg[:, :, :, :], 1e30)
                nc.gpsimd.memset(total[:, :, :, :], 0.0)
                pool.drain().then_inc(cleared, 1)

                def body(pair):
                    for hs in range(2):
                        pool.wait_ge(w_ready, pair.count(2, hs + 1))
                        pool.wait_ge(parted, pair.count(2 * NT, NT * (hs + 1)))
                        if hs == 0 and pair.after(1):
                            pool.wait_ge(o_out, pair.count(16, 0))
                        for c in range(NC):
                            n = NT - CK * c
                            wc = w[:, hs, c, CK * c:NT].unsqueeze(2).to_broadcast([P, n, HD])
                            nc.gpsimd.tensor_tensor(acc[:, :, :] if c == 0 else tmp[:, 0:n, :], part[:, hs, c, CK * c:NT, :], wc, ALU.mult)
                            pool.drain()
                            if c > 0:
                                a = acc[:, CK * c:NT, :]
                                nc.gpsimd.tensor_tensor(a, a, tmp[:, 0:n, :], ALU.add)
                                pool.drain()
                        nc.gpsimd.tensor_copy(o[:, :, hs, :], acc[:, :, :])
                        pool.drain().then_inc(combined, 1)
                pairs(pool, body)

            def weigh_at():
                return {NU + 8: 0, PU + 2: 1}

            def copy_flipped(eng, copy, pair, u, done):
                hs, t, c, lo, n, pieces = pair_units[u]
                eng.wait_ge(flipped, pair.count(PU, u + 1))
                if pair.after(1) or u >= 3:
                    eng.wait_ge(summed, pair.count(PU, u - 2))
                first = 1 if c == 0 else 0
                last = None
                if c == 0:
                    last = copy(pT[0:META, u % 3, 0:P], PT[0:META, u % 3, 0:P])
                if len(pieces) > first:
                    last = copy(pT[:, u % 3, P * first:P * len(pieces)], PT[:, u % 3, P * first:P * len(pieces)])
                if c == 0 and len(pieces) > 1:
                    last = eng.drain()
                last.then_inc(done, 1)

            @block.scalar
            def _(act):
                act.wait_ge(cleared, 1)

                def body(pair):
                    for k in range(PU + 3):
                        if k < PU:
                            hs, t, c, lo, n, pieces = pair_units[k]
                            act.wait_ge(maxed, pair.count(PU, k + 1))
                            if pair.after(1) or k >= 3:
                                act.wait_ge(flipped, pair.count(PU, k - 2))
                            if t == 0 and pair.after(1):
                                act.wait_ge(w_ready, pair.count(2, hs - 1))
                            nc.scalar.activation(prob[:, k % 3, 0:n], S[:, k % 3, 0:n], ACT.Exp, bias=neg[:, hs, c, t:t + 1], scale=B_SCALE,
                                                 accum_out=total[:, hs, c, t:t + 1]).then_inc(exped, 1)
                        u = k - 2
                        if 0 <= u < PU and u % 2:
                            copy_flipped(act, nc.scalar.copy, pair, u, pT_act)
                        if k in weigh_at():
                            hs = weigh_at()[k]
                            act.wait_ge(w_in, pair.count(2, hs + 1))
                            nc.scalar.activation(w[:, hs, :, :], w[:, hs, :, :], ACT.Exp)
                            act.drain().then_inc(w_exped, 1)
                pairs(act, body)

            @block.vector
            def _(dve):
                dve.wait_ge(cleared, 1)

                def take_products(pair, u):
                    hs, t, c, lo, n, pieces = pair_units[u]
                    if c != chunks_of[t] - 1:
                        return
                    dve.wait_ge(summed, pair.count(PU, u + 1))
                    if t == 0 and pair.after(1):
                        dve.wait_ge(combined, pair.count(2, hs - 1))
                    nc.vector.tensor_copy(part[:, hs, 0:c + 1, t, :], O[:, t % 2 if hs == 0 else (NT + t) % 2, 0:HD * (c + 1)]
                                          .rearrange("p (c d) -> p c d", d=HD)).then_inc(parted, 1)

                def weigh(pair, hs):
                    dve.wait_ge(exped, pair.count(PU, NU * (hs + 1)))
                    if pair.after(1):
                        dve.wait_ge(combined, pair.count(2, hs - 1))
                    nc.vector.tensor_reduce(low[:, :], neg[:, hs, :, :].rearrange("p c t -> p t c"), axis=AX.X, op=ALU.min)
                    dve.drain()
                    nc.vector.tensor_tensor(w[:, hs, :, :], low[:, :].unsqueeze(1).to_broadcast([P, NC, NT]), neg[:, hs, :, :], ALU.subtract)
                    dve.drain().then_inc(w_in, 1)
                    dve.wait_ge(w_exped, pair.count(2, hs + 1))
                    nc.vector.tensor_tensor(wt[:, :, :], w[:, hs, :, :], total[:, hs, :, :], ALU.mult)
                    dve.drain()
                    nc.vector.reduce_sum(den[:, :], wt[:, :, :].rearrange("p c t -> p t c"), AX.X)
                    dve.drain()
                    nc.vector.reciprocal(den[:, :], den[:, :])
                    dve.drain()
                    nc.vector.tensor_tensor(w[:, hs, :, :], w[:, hs, :, :], den[:, :].unsqueeze(1).to_broadcast([P, NC, NT]), ALU.mult)
                    dve.drain().then_inc(w_ready, 1)

                def body(pair):
                    for k in range(PU + 5):
                        if k < PU:
                            hs, t, c, lo, n, pieces = pair_units[k]
                            dve.wait_ge(scored, pair.count(PU, k + 1))
                            nc.vector.reduce_max(mx[:, k % 3:k % 3 + 1], S[:, k % 3, 0:n], AX.X)
                            dve.drain()
                            nc.vector.tensor_scalar(neg[:, hs, c, t:t + 1], mx[:, k % 3:k % 3 + 1], -B_SCALE, None, ALU.mult).then_inc(maxed, 1)
                        u = k - 2
                        if 0 <= u < PU and u % 2 == 0:
                            copy_flipped(dve, nc.vector.tensor_copy, pair, u, pT_dve)
                        if k >= 5:
                            take_products(pair, k - 5)
                        if k in weigh_at():
                            weigh(pair, weigh_at()[k])
                pairs(dve, body)

            @block.tensor
            def _(pe):
                pe.wait_ge(consts, 16 * NCONST)

                def body(pair):
                    for k in range(PU + 4):
                        if k < PU:
                            hs, t, c, lo, n, pieces = pair_units[k]
                            if t == 0:
                                pe.wait_ge(qk_in[hs], pair.count(32, 32))
                            if pair.after(1) or k >= 3:
                                pe.wait_ge(exped, pair.count(PU, k - 2))
                            diagonal = c == chunks_of[t] - 1
                            m = nc.tensor.matmul(S[:, k % 3, 0:n], qT[:, hs, P * t:P * t + P], kT[:, hs, lo:lo + n],
                                                 start=True, stop=not diagonal)
                            if diagonal:
                                d = min(P, n)
                                m = nc.tensor.matmul(S[:, k % 3, n - d:n], identb[:, :], mask[:, 0:d], start=False, stop=True)
                            m.then_inc(scored, 1)
                        u = k - 2
                        if 0 <= u < PU:
                            hs, t, c, lo, n, pieces = pair_units[u]
                            pe.wait_ge(exped, pair.count(PU, u + 1))
                            if pair.after(1) or u >= 3:
                                pe.wait_ge(copier(u - 3 if u >= 3 else u - 3 + PU)[0], pair.count(NU, (u - 3) // 2 + 1))
                            for b, (at, keys, tv) in enumerate(pieces):
                                m = nc.tensor.transpose(PT[0:keys, u % 3, P * b:P * b + P], prob[:, u % 3, at:at + keys], ident[:, :])
                            m.then_inc(flipped, 1)
                        u = k - 4
                        if u >= 0:
                            hs, t, c, lo, n, pieces = pair_units[u]
                            sem, count = copier(u)
                            pe.wait_ge(sem, pair.count(NU, count))
                            g = NT * hs + t
                            if t == 0:
                                pe.wait_ge(v_in[hs], pair.count(16, 16))
                            if c == 0 and (pair.after(1) or g >= 2):
                                pe.wait_ge(parted, pair.count(2 * NT, g - 1))
                            for b, (at, keys, tv) in enumerate(pieces):
                                m = nc.tensor.matmul(O[:, g % 2, HD * c:HD * c + HD], pT[0:keys, u % 3, P * b:P * b + P], v[0:keys, hs, tv, :],
                                                     start=(b == 0), stop=(b == len(pieces) - 1))
                            m.then_inc(summed, 1)
                pairs(pe, body)


def experts_beyond(nc, io, dram, keep, layer):
    counts = keep["counts"]

    def count(at):
        return nc.values_load(counts[0:1, at], min_val=0, max_val=2 * KEYS)

    with nc.If(count(slice(EXPERTS, EXPERTS + 1)) > 0):
        with nc.Fori(0, EXPERTS) as e:
            n = count(bass.ds(e, 1))
            with nc.If(n > CAP):
                with nc.Fori(0, OVER) as b:
                    with nc.If(n > b * P + CAP):
                        expert_block(nc, io, dram, layer, e, e * STRIDE + b * P + CAP)


def expert_block(nc, io, dram, layer, e, start):
    with ExitStack() as ctx:
        s = Space(nc, ctx, f"eb{layer}")
        ident = s.sb("ident", [P, P])
        wg = s.sb("wg", [P, DC, FE])
        wu = s.sb("wu", [P, DC, FE])
        wd = s.sb("wd", [P, FC, D])
        slot = s.sb("slot", [P, 2], I32)
        x = s.sb("x", [P, D])
        xT = s.sb("xT", [P, DC, P])
        act_g = s.sb("act_g", [P, FC, P])
        hT = s.sb("hT", [P, FC, P])
        y = s.sb("y", [P, D])
        T = s.ps("T", [P, 2, 512])
        G = s.ps("G", [P, 512])
        U = s.ps("U", [P, 512])
        Y = s.ps("Y", [P, 2, 512])
        ident_in, slot_in, gu_in, d_in, x_in = (s.sem(n) for n in ("ident_in", "slot_in", "gu_in", "d_in", "x_in"))
        flipped, copied, gated, silued, h_ready, downed, y_ready, y_out = (
            s.sem(n) for n in ("flipped", "copied", "gated", "silued", "h_ready", "downed", "y_ready", "y_out"))

        def of_expert(t):
            return t[bass.ds(e, 1)].rearrange("a p n -> (a p) n")

        with nc.Block() as block:
            @block.sync
            def _(sp):
                sp.dma_start(slot[:, :], dram["slot"][bass.ds(start, P), :]).then_inc(slot_in, 16)
                sp.dma_start(ident[:, :], io["ident"]).then_inc(ident_in, 16)
                for w, name in ((wg, "moe_w_gate"), (wu, "moe_w_up")):
                    sp.dma_start(w[:, :, :].rearrange("p c f -> p (c f)"),
                                 of_expert(io[name][layer].rearrange("e (p c) f -> e p (c f)", c=DC))).then_inc(gu_in, 16)
                sp.dma_start(wd[:, :, :].rearrange("p c f -> p (c f)"),
                             of_expert(io["moe_w_down"][layer].rearrange("e (p c) f -> e p (c f)", c=FC))).then_inc(d_in, 16)

            @block.gpsimd
            def _(pool):
                pool.wait_ge(slot_in, 16)
                pool.indirect_dma_start(x[:, :], None, dram["xn"], bass.IndirectOffsetOnAxis(ap=slot[:, 0:1], axis=0)).then_inc(x_in, 16)
                pool.wait_ge(y_ready, 2)
                pool.indirect_dma_start(dram["y"], bass.IndirectOffsetOnAxis(ap=slot[:, 1:2], axis=0), y[:, :], None,
                                        bounds_check=2 * ROWS - 1, oob_is_err=False).then_inc(y_out, 16)
                pool.wait_ge(y_out, 16)

            @block.scalar
            def _(act):
                for b in range(2):
                    act.wait_ge(flipped, b + 1)
                    nc.scalar.copy(xT[:, 4 * b:4 * b + 4, :].rearrange("p c t -> p (c t)"), T[:, b, :]).then_inc(copied, 1)
                act.wait_ge(gated, 1)
                nc.scalar.activation(act_g[:, :, :].rearrange("p c t -> p (c t)"), G[:, 0:FC * P], ACT.Silu).then_inc(silued, 1)
                act.wait_ge(downed, 1)
                nc.scalar.copy(y[:, 0:512], Y[:, 0, :]).then_inc(y_ready, 1)

            @block.vector
            def _(dve):
                dve.wait_ge(silued, 1)
                nc.vector.tensor_tensor(hT[:, :, :].rearrange("p c t -> p (c t)"), act_g[:, :, :].rearrange("p c t -> p (c t)"),
                                        U[:, 0:FC * P], ALU.mult).then_inc(h_ready, 1)
                dve.wait_ge(downed, 2)
                nc.vector.tensor_copy(y[:, 512:D], Y[:, 1, :]).then_inc(y_ready, 1)

            @block.tensor
            def _(pe):
                pe.wait_ge(ident_in, 16)
                pe.wait_ge(x_in, 16)
                for b in range(2):
                    for c in range(4 * b, 4 * b + 4):
                        last = nc.tensor.transpose(T[:, b, P * (c % 4):P * (c % 4) + P],
                                                   x[:, :].rearrange("p (q c) -> p c q", c=DC)[:, c, :], ident[:, :])
                    last.then_inc(flipped, 1)
                pe.wait_ge(gu_in, 32)
                pe.wait_ge(copied, 2)
                for w, out in ((wg, G), (wu, U)):
                    for k in range(FC):
                        for c in range(DC):
                            last = nc.tensor.matmul(out[:, P * k:P * k + P], w[:, c, :].rearrange("p (q k) -> p k q", k=FC)[:, k, :], xT[:, c, :],
                                                    start=(c == 0), stop=(c == DC - 1))
                last.then_inc(gated, 1)
                pe.wait_ge(d_in, 16)
                pe.wait_ge(h_ready, 1)
                for b in range(2):
                    for k in range(FC):
                        last = nc.tensor.matmul(Y[:, b, :], hT[:, k, :], wd[:, k, 512 * b:512 * b + 512], start=(k == 0), stop=(k == FC - 1))
                    last.then_inc(downed, 1)


def finish(nc, io, dram, keep, out):
    with ExitStack() as ctx:
        s = Space(nc, ctx, "fi")
        gain = s.sb("gain", [P, D])
        half = s.sb("half", [P, 1])
        h = s.sb("h", [P, 4, D])
        y = s.sb("y", [P, 4, 2, D])
        hsq = s.sb("hsq", [P, D])
        ssq = s.sb("ssq", [P, 2])
        rstd = s.sb("rstd", [P, 2])
        xn = s.sb("xn", [P, 2, D])
        consts = s.sem("consts")
        h_in = s.sems("h_in", 4)
        y_in = s.sems("y_in", 4)
        held = s.sem("held")
        summed = s.sem("summed")
        squared = s.sem("squared")
        rstd_ready = s.sem("rstd_ready")
        xn_ready = s.sem("xn_ready")
        xn_out = s.sems("xn_out", 2)
        NB = NT - 1

        with nc.Block() as block:
            @block.sync
            def _(sp):
                sp.dma_start(gain[:, :], bcast(io["final_norm"], D)).then_inc(consts, 16)

                def load(i):
                    if i.after(4):
                        sp.wait_ge(xn_ready, i.back(4).count(1, 1))
                    sp.dma_start(h[:, i.slot4, :], rows(dram["h"], i.back(-1))).then_inc(h_in[i.slot4], 16)
                    sp.dma_start(y[:, i.slot4, :, :].rearrange("p k d -> p (k d)"),
                                 rows(dram["y"].rearrange("(r k) d -> r (k d)", k=2), i.back(-1))).then_inc(y_in[i.slot4], 16)

                def step(i):
                    if i.turn is None and i.c == 0:
                        for k in range(3):
                            load(i.back(-k))
                    if i.back(-3).live(NB):
                        load(i.back(-3))
                    j = i.back(1)
                    if j.live(NB):
                        sp.wait_ge(xn_ready, j.count(1, 1))
                        sp.dma_start(rows(out, j), xn[:, j.slot, :]).then_inc(xn_out[j.slot], 16)
                over_steps(sp, 0, 1 + NB, 4, NB - 4, step, unroll=4)
                for b in range(2):
                    sp.wait_ge(xn_out[b], 16 * (NB // 2))

            @block.gpsimd
            def _(pool):
                nc.gpsimd.memset(half[:, :], -0.5)
                pool.drain()

                def step(i):
                    pool.wait_ge(squared, i.count(1, 1))
                    pool.sem_inc(held, 1)
                    nc.gpsimd.tensor_scalar(rstd[:, i.slot:i.slot + 1], ssq[:, i.slot:i.slot + 1], 1.0 / D, EPS, ALU.mult, ALU.add)
                    pool.drain()
                    nc.gpsimd.tensor_tensor(rstd[:, i.slot:i.slot + 1], rstd[:, i.slot:i.slot + 1], half[:, :], ALU.pow).then_inc(rstd_ready, 1)
                over_steps(pool, 0, NB, 4, NB, step, unroll=4)

            @block.scalar
            def _(act):
                def step(i):
                    act.wait_ge(summed, i.count(1, 1))
                    nc.scalar.activation(hsq[:, :], h[:, i.slot4, :], ACT.Square, accum_out=ssq[:, i.slot:i.slot + 1])
                    act.drain().then_inc(squared, 1)
                over_steps(act, 0, NB, 4, NB, step, unroll=4)

            @block.vector
            def _(dve):
                dve.wait_ge(consts, 16)

                def step(i):
                    if i.live(NB):
                        dve.wait_ge(h_in[i.slot4], (i.uses4 + 1) * 16)
                        dve.wait_ge(y_in[i.slot4], (i.uses4 + 1) * 16)
                        for k in range(2):
                            w = keep["weights"][:, :, k]
                            w = w[:, i.c + 1:i.c + 2] if i.turn is None else w[:, bass.ds(i.n + 1, 1)]
                            nc.vector.scalar_tensor_tensor(out=h[:, i.slot4, :], in0=y[:, i.slot4, k, :], scalar=w, in1=h[:, i.slot4, :],
                                                           op0=ALU.mult, op1=ALU.add)
                            if k == 0:
                                dve.drain()
                        dve.drain().then_inc(summed, 1)
                    j = i.back(1)
                    if j.live(NB):
                        dve.wait_ge(rstd_ready, j.count(1, 1))
                        if j.after(2):
                            dve.wait_ge(xn_out[j.slot], j.uses * 16)
                        nc.vector.scalar_tensor_tensor(out=xn[:, j.slot, :], in0=h[:, j.slot4, :], scalar=rstd[:, j.slot:j.slot + 1],
                                                       in1=gain[:, :], op0=ALU.mult, op1=ALU.mult).then_inc(xn_ready, 1)
                over_steps(dve, 0, 1 + NB, 4, NB, step, unroll=4)


def program(nc, io, out):
    dram = {}

    def scratch(name, shape, dt=F32):
        dram[name] = nc.dram_tensor(f"scratch_{name}", shape, dt, kind="Internal").ap()
    scratch("o", (ROWS, D))
    scratch("h", (ROWS, D))
    scratch("xn", (ROWS + P, D))
    scratch("slot", (SLOTS, 2), I32)
    scratch("y", (2 * ROWS, D))
    scratch("qT", (HEADS, QD, ROWS))
    scratch("kT", (HEADS, HD, KEYS))
    scratch("kpeT", (ROPE, KEYS))
    scratch("v", (HEADS, P, NT, HD))
    with ExitStack() as ctx:
        s = Space(nc, ctx, "keep")
        keep = {"weights": s.sb("weights", [P, NT, 2]), "counts": s.sb("counts", [P, EXPERTS + 1], I32), "bias_in": s.sem("bias_in")}
        attention_a(nc, io, dram)
        project_and_route(nc, io, dram, keep, 0)
        experts(nc, io, dram, keep, 0)
        experts_beyond(nc, io, dram, keep, 0)
        combine_and_project_b(nc, io, dram, keep)
        attention_b(nc, io, dram)
        project_and_route(nc, io, dram, keep, 1)
        experts(nc, io, dram, keep, 1)
        experts_beyond(nc, io, dram, keep, 1)
        finish(nc, io, dram, keep, out.rearrange("o t d -> (o t) d"))


INPUTS = ["x", "meta_tokens", "attn_norm", "ffn_norm", "final_norm", "a_w_qkv", "a_b_qkv", "a_sinks", "a_w_o", "a_b_o",
          "b_w_in", "b_q_norm", "b_kv_norm", "b_w_uq", "b_w_ukv", "b_w_o", "moe_w_group", "moe_b_group",
          "moe_w_router", "moe_b_router", "moe_w_gate", "moe_w_up", "moe_w_down"]


def shape_constants():
    pos = np.zeros((NT, P), np.float32)
    pos[0, :META] = np.arange(META)
    pos[1:] = META + np.arange(SEQ).reshape(NT - 1, P)

    def table(dim):
        inv = (1.0 / (np.float32(10000.0) ** (np.arange(0, dim, 2, dtype=np.float32) / np.float32(dim)))).astype(np.float32)
        ang = (pos.reshape(-1, 1) * inv[None, :]).astype(np.float32)
        cos, sin = np.cos(ang).astype(np.float32), np.sin(ang).astype(np.float32)
        return np.concatenate([cos, cos, -sin, sin], axis=1)

    bf = np.dtype("bfloat16")
    q, k = np.arange(P)[:, None], np.arange(P)[None, :]
    mask = np.full((NT, P, BAND), MASKED, np.float32)
    mask[1:, :, 0:META] = 0
    mask[2:, :, META:META + P] = np.where(k > q, 0, MASKED)
    mask[:, :, META + P:] = np.where(k <= q, 0, MASKED)
    pad = (np.arange(ROWS) >= META) & (np.arange(ROWS) < P)
    info = np.zeros((ROWS, 7), np.float32)
    info[:, 0] = 1 - pad
    info[:, 1] = np.where(pad, EXPERTS * STRIDE + np.arange(ROWS) % P, 0)
    info[:, 2] = np.where(pad, EXPERTS * STRIDE + P + np.arange(ROWS) % P, 0)
    info[:, 3] = info[:, 5] = np.arange(ROWS)
    info[:, 4], info[:, 6] = 2 * np.arange(ROWS), 2 * np.arange(ROWS) + 1
    return {
        "ident": np.eye(P, dtype=np.float32),
        "identb": np.eye(P).astype(bf),
        "cs_a": table(HD),
        "cs_b": table(ROPE),
        "mask_a": mask.reshape(ROWS, BAND).astype(bf),
        "mask_b": np.where(k <= q, 0, MASKED).astype(bf),
        "ones_tri": np.concatenate([(q < k).astype(np.float32), np.ones((P, P), np.float32)], axis=1).astype(bf),
        "iota": np.tile(np.arange(EXPERTS, dtype=np.float32), (P, 1)),
        "base": np.tile(np.arange(EXPERTS, dtype=np.float32) * STRIDE, (P, 1)),
        "info": info,
    }


def kernel(**inputs):
    import concourse.bacc as bacc
    from concourse.bass_utils import run_bass_kernel_spmd as run

    nc = bacc.Bacc("TRN2", target_bir_lowering=False, num_devices=1)
    arrays = {name: np.ascontiguousarray(inputs[name]) for name in INPUTS}
    arrays["x"] = arrays["x"].reshape(SEQ, D)
    arrays.update(shape_constants())
    arrays = {f"in_{k}": a for k, a in arrays.items()}
    io = {k[3:]: nc.dram_tensor(k, a.shape, mybir.dt.from_np(a.dtype), kind="ExternalInput").ap() for k, a in arrays.items()}
    out = nc.dram_tensor("out", (1, SEQ, D), F32, kind="ExternalOutput").ap()
    program(nc, io, out)
    r = run(nc, [arrays], core_ids=[0])
    return r.results[0]["out"]
```
